# Optimizing a Trainium2 kernel written in Bass

```python
import math
import jax, jax.numpy as jnp
from jax import lax
import numpy as np

D_MODEL = 1024
BATCH = 1
SEQ = 256
DEPTH = 2

CHUNK = 64
GDN_HEADS = 4
GDN_DK = 128
GDN_DV = 128
CONV_WIDTH = 4
SWA_HEADS = 8
SWA_KV_HEADS = 2
SWA_DH = 64
SWA_WINDOW = 128
SWA_ROT_DIM = SWA_DH // 4
ROPE_THETA = 500000.0
RET_HEADS = 4
RET_DK = 256
RET_DV = 512
RET_THETA = 10000.0
FFN_DENSE = 2816
N_EXPERTS = 8
TOP_K = 2
FFN_EXPERT = 3584
ALPHA = (2.0 * DEPTH) ** 0.25
BETA = (8.0 * DEPTH) ** -0.25
LN_EPS = 1e-5
NORM_EPS = 1e-6
MASK_VALUE = -1e30
A_QK = GDN_HEADS * GDN_DK
A_V = GDN_HEADS * GDN_DV
B_Q = SWA_HEADS * SWA_DH
B_KV = SWA_KV_HEADS * SWA_DH
EVEN_WIDTHS = (2 * A_QK + A_V, A_V, GDN_HEADS, GDN_HEADS, B_Q, B_KV, B_KV)
EVEN_PROJ = 2 * A_QK + 2 * A_V + 2 * GDN_HEADS + B_Q + 2 * B_KV
D_MIX_EVEN = A_V + B_Q
RET_QK = RET_HEADS * RET_DK
RET_V = RET_HEADS * RET_DV
ODD_WIDTHS = (RET_QK, RET_QK, RET_V, RET_V)
ODD_PROJ = 2 * RET_QK + 2 * RET_V

kernel_name = "hybrid_gdn_swa_retention_moe_block"

def split_cols(t, widths):
    return jnp.split(t, np.cumsum(widths)[:-1].tolist(), axis=-1)

def layer_norm(x, w, b):
    xf = x.astype(jnp.float32)
    mu = xf.mean(-1, keepdims=True)
    var = jnp.square(xf - mu).mean(-1, keepdims=True)
    return ((xf - mu) * lax.rsqrt(var + LN_EPS) * w.astype(jnp.float32) + b.astype(jnp.float32)).astype(x.dtype)

def rms_norm(x, w):
    xf = x.astype(jnp.float32)
    return xf * lax.rsqrt(jnp.mean(xf * xf, -1, keepdims=True) + NORM_EPS) * w.astype(jnp.float32)

def l2_normalize(x):
    xf = x.astype(jnp.float32)
    return xf * lax.rsqrt(jnp.sum(xf * xf, -1, keepdims=True) + NORM_EPS)

def rotary(x, positions, rot_dim, theta):
    half = rot_dim // 2
    inv_freq = theta ** (-jnp.arange(half, dtype=jnp.float32) / half)
    ang = positions.astype(jnp.float32)[..., None] * inv_freq
    cos, sin = jnp.cos(ang)[:, :, None, :], jnp.sin(ang)[:, :, None, :]
    xr = x[..., :rot_dim].astype(jnp.float32)
    x1, x2 = xr[..., :half], xr[..., half:]
    rot = jnp.concatenate([x1 * cos - x2 * sin, x2 * cos + x1 * sin], -1).astype(x.dtype)
    return jnp.concatenate([rot, x[..., rot_dim:]], -1)

def causal_conv(x, w):
    k_w, s = w.shape[0], x.shape[1]
    xp = jnp.pad(x, ((0, 0), (k_w - 1, 0), (0, 0)))
    return sum(xp[:, j:j + s] * w[j] for j in range(k_w))

def to_chunks(t):
    b, s = t.shape[:2]
    t = t.reshape((b, s // CHUNK, CHUNK) + t.shape[2:])
    return jnp.moveaxis(t, 3, 2)

def from_chunks(t):
    t = jnp.moveaxis(t, 2, 3)
    return t.reshape((t.shape[0], t.shape[1] * CHUNK) + t.shape[3:])

def gated_delta_rule(q, k, v, g, beta):
    f32 = jnp.float32
    q, k, v = (to_chunks(t.astype(f32)) for t in (q, k, v))
    g, beta = to_chunks(g.astype(f32)), to_chunks(beta.astype(f32))
    b_, _, h_, _, dk = q.shape
    dv = v.shape[-1]
    q = q * dk ** -0.5
    G = jnp.cumsum(g, axis=-1)
    tril = jnp.tril(jnp.ones((CHUNK, CHUNK), bool))
    strict = jnp.tril(jnp.ones((CHUNK, CHUNK), bool), -1)
    diff = G[..., :, None] - G[..., None, :]
    decay = jnp.where(tril, jnp.exp(jnp.where(tril, diff, 0.0)), 0.0)
    kb = k * beta[..., None]
    a = jnp.where(strict, jnp.einsum('bnhid,bnhjd->bnhij', kb, k) * decay, 0.0)
    t_mat = a + jnp.eye(CHUNK, dtype=f32)
    rhs = jnp.concatenate([v * beta[..., None], kb * jnp.exp(G)[..., None]], -1)
    sol = lax.linalg.triangular_solve(t_mat, rhs, left_side=True, lower=True, unit_diagonal=True)
    u, w = sol[..., :dv], sol[..., dv:]
    qk = jnp.where(tril, jnp.einsum('bnhid,bnhjd->bnhij', q, k) * decay, 0.0)
    q_dec = q * jnp.exp(G)[..., None]
    k_dec = k * jnp.exp(G[..., -1:] - G)[..., None]
    chunk_decay = jnp.exp(G[..., -1])

    def step(state, inp):
        q_c, k_c, u_c, w_c, qk_c, cd = inp
        v_new = u_c - jnp.einsum('bhcd,bhde->bhce', w_c, state)
        o = jnp.einsum('bhcd,bhde->bhce', q_c, state) + jnp.einsum('bhij,bhje->bhie', qk_c, v_new)
        state = state * cd[..., None, None] + jnp.einsum('bhcd,bhce->bhde', k_c, v_new)
        return state, o

    xs = tuple(jnp.moveaxis(t, 1, 0) for t in (q_dec, k_dec, u, w, qk, chunk_decay))
    _, o = lax.scan(step, jnp.zeros((b_, h_, dk, dv), f32), xs)
    return from_chunks(jnp.moveaxis(o, 0, 1))

def sink_window_attention(q, k, v, sinks):
    b_, s, hq, d = q.shape
    hkv = k.shape[2]
    grp = hq // hkv
    n = s // CHUNK
    nb = SWA_WINDOW // CHUNK
    qb = q.reshape(b_, n, CHUNK, hkv, grp, d)

    def band(t):
        tc = jnp.pad(t.reshape(b_, n, CHUNK, hkv, d), ((0, 0), (nb - 1, 0), (0, 0), (0, 0), (0, 0)))
        return jnp.concatenate([tc[:, j:j + n] for j in range(nb)], axis=2)

    kband, vband = band(k), band(v)
    key_chunk = jnp.arange(n)[:, None] - (nb - 1) + (jnp.arange(nb * CHUNK) // CHUNK)[None, :]
    valid = key_chunk >= 0
    sc = jnp.einsum('bnqhgd,bnkhd->bnhgqk', qb, kband).astype(jnp.float32) * d ** -0.5
    sc = jnp.where(valid[None, :, None, None, None, :], sc, MASK_VALUE)
    sink = sinks.astype(jnp.float32).reshape(hkv, grp)[None, None, :, :, None, None]
    m = jnp.maximum(sc.max(-1, keepdims=True), sink)
    p = jnp.exp(sc - m)
    probs = p / (p.sum(-1, keepdims=True) + jnp.exp(sink - m))
    o = jnp.einsum('bnhgqk,bnkhd->bnqhgd', probs.astype(v.dtype), vband)
    return o.reshape(b_, s, hq, d)

def multiscale_retention(q, k, v):
    f32 = jnp.float32
    q, k, v = (to_chunks(t.astype(f32)) for t in (q, k, v))
    b_, _, h_, _, dk = q.shape
    dv = v.shape[-1]
    k = k * dk ** -0.5
    log_g = jnp.log1p(-jnp.exp2(-5.0 - jnp.arange(h_, dtype=f32)))
    idx = jnp.arange(CHUNK, dtype=f32)
    dist = idx[:, None] - idx[None, :]
    d_mask = jnp.where(dist >= 0, jnp.exp(jnp.maximum(dist, 0.0) * log_g[:, None, None]), 0.0)
    o_intra = jnp.einsum('bnhij,bnhje->bnhie', jnp.einsum('bnhid,bnhjd->bnhij', q, k) * d_mask, v)
    xi = jnp.exp((idx + 1.0) * log_g[:, None])
    zeta = jnp.exp((CHUNK - 1.0 - idx) * log_g[:, None])
    chunk_decay = jnp.exp(CHUNK * log_g)
    q_dec = q * xi[:, :, None]
    k_dec = k * zeta[:, :, None]

    def step(r, inp):
        q_c, k_c, v_c = inp
        o = jnp.einsum('bhcd,bhde->bhce', q_c, r)
        r = r * chunk_decay[:, None, None] + jnp.einsum('bhcd,bhce->bhde', k_c, v_c)
        return r, o

    xs = tuple(jnp.moveaxis(t, 1, 0) for t in (q_dec, k_dec, v))
    _, o_inter = lax.scan(step, jnp.zeros((b_, h_, dk, dv), f32), xs)
    return from_chunks(o_intra + jnp.moveaxis(o_inter, 0, 1))

def even_mixer(h, positions, w_in, conv_w, a_log, dt_bias, gdn_norm_w, sinks, w_out):
    b_, s, _ = h.shape
    a_qkv, a_z, a_a, a_b, b_q, b_k, b_v = split_cols(h @ w_in, EVEN_WIDTHS)
    a_qkv = jax.nn.silu(causal_conv(a_qkv, conv_w))
    a_q, a_k, a_v = split_cols(a_qkv, (A_QK, A_QK, A_V))
    a_q = l2_normalize(a_q.reshape(b_, s, GDN_HEADS, GDN_DK))
    a_k = l2_normalize(a_k.reshape(b_, s, GDN_HEADS, GDN_DK))
    a_v = a_v.reshape(b_, s, GDN_HEADS, GDN_DV)
    g = -jnp.exp(a_log.astype(jnp.float32)) * jax.nn.softplus(a_a.astype(jnp.float32) + dt_bias.astype(jnp.float32))
    beta = jax.nn.sigmoid(a_b.astype(jnp.float32))
    o_a = gated_delta_rule(a_q, a_k, a_v, g, beta)
    o_a = rms_norm(o_a, gdn_norm_w) * jax.nn.silu(a_z.reshape(b_, s, GDN_HEADS, GDN_DV).astype(jnp.float32))
    q = rotary(b_q.reshape(b_, s, SWA_HEADS, SWA_DH), positions, SWA_ROT_DIM, ROPE_THETA)
    k = rotary(b_k.reshape(b_, s, SWA_KV_HEADS, SWA_DH), positions, SWA_ROT_DIM, ROPE_THETA)
    v = b_v.reshape(b_, s, SWA_KV_HEADS, SWA_DH)
    o_b = sink_window_attention(q, k, v, sinks)
    o = jnp.concatenate([o_a.reshape(b_, s, A_V).astype(h.dtype), o_b.reshape(b_, s, B_Q).astype(h.dtype)], -1)
    return o @ w_out

def retention_mixer(h, positions, w_in, gn_w, w_out):
    b_, s, _ = h.shape
    q, k, v, g = split_cols(h @ w_in, ODD_WIDTHS)
    q = rotary(q.reshape(b_, s, RET_HEADS, RET_DK), positions, RET_DK, RET_THETA)
    k = rotary(k.reshape(b_, s, RET_HEADS, RET_DK), positions, RET_DK, RET_THETA)
    y = multiscale_retention(q, k, v.reshape(b_, s, RET_HEADS, RET_DV))
    mu = y.mean(-1, keepdims=True)
    var = jnp.square(y - mu).mean(-1, keepdims=True)
    y = (y - mu) * lax.rsqrt(var + NORM_EPS) * gn_w.astype(jnp.float32).reshape(RET_HEADS, RET_DV)
    y = jax.nn.silu(g.astype(jnp.float32)) * y.reshape(b_, s, RET_V)
    return y.astype(h.dtype) @ w_out

def swiglu(h, w_up, w_down):
    gate, up = jnp.split(h @ w_up, 2, axis=-1)
    return (jax.nn.silu(gate) * up) @ w_down

def moe_swiglu(h, w_router, b_router, w_up, w_down):
    b_, s, d = h.shape
    t = h.reshape(b_ * s, d)
    logits = (t @ w_router).astype(jnp.float32) + b_router.astype(jnp.float32)
    top_vals, top_idx = lax.top_k(logits, TOP_K)
    weights = jax.nn.softmax(top_vals, axis=-1)
    combine = jnp.sum(jax.nn.one_hot(top_idx, N_EXPERTS, dtype=jnp.float32) * weights[..., None], axis=1)
    out = jnp.zeros_like(t)
    for e in range(N_EXPERTS):
        out = out + combine[:, e:e + 1].astype(t.dtype) * swiglu(t, w_up[e], w_down[e])
    return out.reshape(b_, s, d)

def setup_inputs(seed: int = 0) -> dict:
    key = jax.random.key(seed)
    ks = jax.random.split(key, 24)
    f32 = jnp.float32
    d = D_MODEL
    ne, no = (DEPTH + 1) // 2, DEPTH // 2

    def nrm(k, shape, scale):
        return jax.random.normal(k, shape, f32) * scale

    ev_col = jnp.asarray(np.concatenate([
        np.ones(2 * A_QK), np.full(A_V, BETA), np.ones(A_V + 2 * GDN_HEADS + B_Q + B_KV), np.full(B_KV, BETA)
    ]).astype(np.float32))
    od_col = jnp.asarray(np.concatenate([np.ones(2 * RET_QK), np.full(RET_V, BETA), np.ones(RET_V)]).astype(np.float32))
    offset = jax.random.randint(ks[2], (BATCH, 1), 0, 256, dtype=jnp.int32) * CHUNK
    dt = jnp.exp(jax.random.uniform(ks[10], (ne, GDN_HEADS), f32, math.log(1e-3), math.log(1e-1)))
    return {
        "x": nrm(ks[0], (BATCH, SEQ, d), 1.0),
        "c": nrm(ks[1], (BATCH, d), 1.0),
        "positions": (offset + jnp.arange(SEQ, dtype=jnp.int32)[None, :]).astype(jnp.int32),
        "cond_w": nrm(ks[3], (DEPTH, d, 6 * d), 0.5 * d ** -0.5),
        "cond_b": nrm(ks[4], (DEPTH, 6 * d), 0.02),
        "ln_w": 1.0 + nrm(ks[5], (DEPTH, 2, d), 0.05),
        "ln_b": nrm(ks[6], (DEPTH, 2, d), 0.02),
        "ev_w_in": nrm(ks[7], (ne, d, EVEN_PROJ), d ** -0.5) * ev_col,
        "ev_conv_w": nrm(ks[8], (ne, CONV_WIDTH, 2 * A_QK + A_V), CONV_WIDTH ** -0.5),
        "ev_a_log": jnp.log(jax.random.uniform(ks[9], (ne, GDN_HEADS), f32, 1.0, 16.0)),
        "ev_dt_bias": dt + jnp.log(-jnp.expm1(-dt)),
        "ev_gdn_norm_w": 1.0 + nrm(ks[11], (ne, GDN_DV), 0.05),
        "ev_sinks": nrm(ks[12], (ne, SWA_HEADS), 0.5),
        "ev_w_out": nrm(ks[13], (ne, D_MIX_EVEN, d), BETA * D_MIX_EVEN ** -0.5),
        "ffn_w_up": nrm(ks[14], (ne, d, 2 * FFN_DENSE), d ** -0.5),
        "ffn_w_down": nrm(ks[15], (ne, FFN_DENSE, d), BETA * FFN_DENSE ** -0.5),
        "od_w_in": nrm(ks[16], (no, d, ODD_PROJ), d ** -0.5) * od_col,
        "od_gn_w": 1.0 + nrm(ks[17], (no, RET_V), 0.05),
        "od_w_out": nrm(ks[18], (no, RET_V, d), BETA * RET_V ** -0.5),
        "moe_w_router": nrm(ks[19], (no, d, N_EXPERTS), d ** -0.5),
        "moe_b_router": nrm(ks[20], (no, N_EXPERTS), 0.01),
        "moe_w_up": nrm(ks[21], (no, N_EXPERTS, d, 2 * FFN_EXPERT), d ** -0.5),
        "moe_w_down": nrm(ks[22], (no, N_EXPERTS, FFN_EXPERT, d), BETA * FFN_EXPERT ** -0.5),
    }

def reference(x, c, positions, cond_w, cond_b, ln_w, ln_b,
              ev_w_in, ev_conv_w, ev_a_log, ev_dt_bias, ev_gdn_norm_w, ev_sinks, ev_w_out,
              ffn_w_up, ffn_w_down,
              od_w_in, od_gn_w, od_w_out,
              moe_w_router, moe_b_router, moe_w_up, moe_w_down):
    c_act = jax.nn.silu(c)
    for layer in range(DEPTH):
        i = layer // 2
        mod = c_act @ cond_w[layer] + cond_b[layer]
        sh_m, sc_m, g_m, sh_f, sc_f, g_f = [m[:, None, :] for m in jnp.split(mod, 6, axis=-1)]
        h = x * (1.0 + sc_m) + sh_m
        if layer % 2 == 0:
            y = even_mixer(h, positions, ev_w_in[i], ev_conv_w[i], ev_a_log[i], ev_dt_bias[i],
                           ev_gdn_norm_w[i], ev_sinks[i], ev_w_out[i])
        else:
            y = retention_mixer(h, positions, od_w_in[i], od_gn_w[i], od_w_out[i])
        x = layer_norm(ALPHA * x + g_m * y, ln_w[layer, 0], ln_b[layer, 0])
        h = x * (1.0 + sc_f) + sh_f
        if layer % 2 == 0:
            y = swiglu(h, ffn_w_up[i], ffn_w_down[i])
        else:
            y = moe_swiglu(h, moe_w_router[i], moe_b_router[i], moe_w_up[i], moe_w_down[i])
        x = layer_norm(ALPHA * x + g_f * y, ln_w[layer, 1], ln_b[layer, 1])
    return x


_drawn_inputs = setup_inputs


def setup_inputs(seed=0):
    import zlib

    import numpy as np

    out = dict(_drawn_inputs(seed))
    spreads = {}
    factors = {'cond_b': 4.262,
     'ev_a_log': 7.036,
     'ev_dt_bias': 3.321,
     'ev_gdn_norm_w': 8.0,
     'ev_sinks': 64.0,
     'od_gn_w': 8.0,
     'moe_b_router': 43.891}
    for name, (base, spread) in spreads.items():
        noise = np.random.default_rng([zlib.crc32(name.encode()), seed]).standard_normal(out[name].shape)
        drawn = base * np.exp(spread * noise) if base else spread * noise
        out[name] = __import__('jax').numpy.asarray(drawn.astype(out[name].dtype))
    for name, factor in factors.items():
        out[name] = (out[name] * factor).astype(out[name].dtype)
    return out
```

```python
from contextlib import ExitStack

import numpy as np

import concourse.bass as bass
from concourse import mybir

ALU = mybir.AluOpType
ACT = mybir.ActivationFunctionType
AX = mybir.AxisListType
F32 = mybir.dt.float32
F32R = mybir.dt.float32r
I32 = mybir.dt.int32

P = 128
D = 1024
SEQ = 256
NT = SEQ // P
KC = D // P
CHUNK = 64
GH, GD = 4, 128
NTH = NT * GH
CONV_W = 4
QKV = 3 * GH * GD
NF = QKV // P
SH, SKV, SD = 8, 2, 64
SG = SH // SKV
SROT = SD // 8
RH, RK, RV = 4, 256, 512
FFN = 2816
NE = 8
FFE = 3584
UNIT = 4096
RING = 3
PIECE = UNIT // 2
ALPHA = 4.0 ** 0.25
LN_EPS = 1e-5
NORM_EPS = 1e-6
NEG = -1e30
N_LEVELS = 6
TWO_PI = 2.0 * np.pi
PI2_A = 6.28125
PI2_B = float(np.float32(np.round((TWO_PI - PI2_A) * 2.0 ** 20) / 2.0 ** 20))
PI2_C = float(np.float32(TWO_PI - PI2_A - PI2_B))
ROUND = 1.5 * 2.0 ** 23
PI_MAX = 3.1415925

NFREQ = RK // 2 + SROT
LATE = ("strict", "iota", "ret")


def constant_table():
    s, t = np.arange(P)[:, None], np.arange(P)[None, :]
    same = (s // CHUNK) == (t // CHUNK)
    parts = {
        "ident": s == t,
        "ones": np.ones((P, P)),
        "upto": (s <= t) & same,
        "after": (s > t) & same,
        "att_own": np.where((s < CHUNK) & (t >= CHUNK), NEG, 0.0),
        "att_prev": np.where((s < CHUNK) & (t >= CHUNK), 0.0, NEG),
        "levels": np.concatenate(
            [((t // b) % 2 == 1) & ((s // b) == (t // b) - 1) for b in (1 << n for n in range(N_LEVELS))], 1
        ),
    }
    half_r, half_s = RK // 2, SROT
    f = np.concatenate([
        np.float32(10000.0) ** (-np.arange(half_r, dtype=np.float32) / np.float32(half_r)),
        np.float32(500000.0) ** (-np.arange(half_s, dtype=np.float32) / np.float32(half_s)),
    ])
    parts["freq"] = np.broadcast_to(f[None, :], (P, NFREQ))
    parts["strict"] = s < t
    parts["iota"] = np.broadcast_to(t, (P, P))
    ret = np.zeros((P, RH, 2, P))
    for h in range(RH):
        log_g = np.log1p(-(2.0 ** (-5.0 - h)))
        dist = (t - s).astype(np.float64)
        ret[:, h, 0] = np.where(dist >= 0, np.exp(np.maximum(dist, 0) * log_g), 0.0)
        ret[:, h, 1] = np.exp((dist + P) * log_g)
    parts["ret"] = ret.reshape(P, -1) * RK ** -0.5
    return parts


def psum_plan(plan):
    at, count, turn = {}, [0] * 8, 0

    def use(*key):
        nonlocal turn
        at[key] = (turn % 8, count[turn % 8])
        count[turn % 8] += 1
        turn += 1

    for key in plan:
        use(*key)
    return at, count


def stream_units():
    c = lambda l, *n: [("cond", l, i) for i in n]
    e = lambda *n: [("ev_in", i) for i in n]
    order = c(0, 0, 1, 2, 3) + e(0) + c(0, 4) + e(1) + c(0, 5) + e(2, 5, 4) + c(0, 6) + e(3)
    order += c(0, 7, 8, 9, 10, 11) + [("ev_out", 0), ("ev_out", 1)]
    for i in range(FFN // 256):
        order += [("ffn_up", i)] + (c(1, i) if i < 10 else [])
    order += [("ffn_down", i) for i in range(6)] + c(1, 10, 11)
    for h in range(RH):
        order += [("od_qk", h), ("od_v", h), ("od_g", h)]
    order += [("od_out", i) for i in range(4)]
    return order


def pe_order():
    o = [("cT",), ("convT",)]
    o += [("cond", 0, u) for u in range(4)] + [("hT", 0, i) for i in range(4)] + [("ab", t) for t in range(NT)]
    for u, c in ((0, 4), (1, 5), (2, None)):
        o += [("ev_in", u, i) for i in range(2)] + ([("cond", 0, c)] if c else [])
    o += [("ev_in", 5, t) for t in range(NT)] + [("ev_in", 4, t) for t in range(NT)] + [("cond", 0, 6)]
    o += [("ev_in", 3, t) for t in range(NT)]
    o += [("l2", i) for i in range(4)]
    o += [("g_row", t) for t in range(NT)] + [("b_row", t) for t in range(NT)] + [("g_after",)]
    o += [("k_tok", t) for t in range(NT)] + [("v_tok", t) for t in range(NT)]
    o += [("kk", t) for t in range(NT)] + [("qk", t) for t in range(NT)]
    o += [("xt", t) for t in range(NT)]
    o += [("att_T", i) for i in range(3)] + [("score", b, v) for b in range(3) for v in range(SKV)]
    for l in range(1, N_LEVELS):
        o += [("ax", l, t) for t in range(NT)]
        o += [("xax", l, t) for t in range(NT)] if l < N_LEVELS - 1 else []
        o += [("yay", l, t) for t in range(NT)] + [("cond", 0, 6 + l)]
    o += [("u", t) for t in range(NT)] + [("w", t) for t in range(NT)]
    o += [("prob_T", b, v) for b in range(3) for v in range(SKV)] + [("pv", t) for t in range(NT)]
    for n in range(4):
        o += ([("ws", n)] if n else []) + ([("kv", n)] if n < 3 else [])
    o += [("go", t) for t in range(NT)]
    o += [("hT", 1, i) for i in range(4)]
    o += [("ev_out", u, t) for u in range(2) for t in range(NT)]
    o += [("hT", 2, i) for i in range(4)]
    for u in range(FFN // 256):
        o += [("ffn_up", u, t) for t in range(NT)] + ([("cond", 1, u - 1)] if 1 <= u <= 10 else [])
        o += [("ffn_T", u - 1)] if u else []
    o += [("ffn_T", FFN // 256 - 1)]
    o += [("ffn_down", t, h) for t in range(NT) for h in range(2)]
    o += [("hT", 3, i) for i in range(4)] + [("cond", 1, 10), ("cond", 1, 11)]
    for h in range(RH + 1):
        if h < RH:
            o += [("od_qk", h, t) for t in range(NT)]
        if h:
            o += [("ret_y", h - 1, t) for t in range(NT)]
        if h < RH:
            o += [("od_v", h, t) for t in range(NT)] + [("ret_T", h, t) for t in range(NT)]
            o += [("od_g", h, t) for t in range(NT)] + [("ret_s", h)]
        if h:
            o += [("ret_yT", h - 1, t) for t in range(NT)]
    o += [("od_out", t, h) for t in range(NT) for h in range(2)]
    o += [("hT", 4, i) for i in range(4)]
    o += [("router",), ("rank",)]
    o += [("gather", 0), ("gather", 1)]
    return o


N_UP = FFE // 256
N_DOWN = FFE // P // 4
N_UNITS = N_UP + N_DOWN
MAX_OVER = 2 * SEQ // (P + 1)
N_ITEMS = NE + MAX_OVER


def item_plan():
    at, count = {}, [0] * 8

    def use(bank, *key):
        at[key] = (bank, count[bank])
        count[bank] += 1

    for u in range(N_UP):
        use(u % 3, "up", u)
        if u:
            use(3 + (u - 1) % 2, "act_T", u - 1)
        else:
            for i in range(4):
                use((6, 3, 4, 5)[i], "back", i)
            use(7, "pwT")
    use(3 + (N_UP - 1) % 2, "act_T", N_UP - 1)
    use(7, "down", 0)
    use(5, "down", 1)
    use(6, "gather", 0)
    use(2, "gather", 1)
    return at, count


class Steps:

    def __init__(self, eng, sem):
        self.eng, self.sem, self.n, self.base = eng, sem, 0, None

    def do(self, ins):
        ins.then_inc(self.sem, 1)
        self.n += 1
        return self.n

    def wait(self, n=None):
        n = self.n if n is None else n
        self.eng.wait_ge(self.sem, n if self.base is None else self.base + n)

    def then(self, ins):
        self.do(ins)
        self.wait()


SEMS = (
    "consts_in x_in c_in convw_in abw_in gates_in sinks_in bias_in gdnw_in ln_in gnw_in ret_in router_in late_in "
    "c_act pads_zero angle_ready trig_ready cond_acc h_ready gate_in gate_exp conv_done q_act k_act v_act squared "
    "qk_norm rope_done k_raw g_rhs b_rhs exp_row dec_exp e_col q_dec level_mask y0_ready score_sub sink_sub "
    "prob_exp sink_exp v_first ssq_ready o_rstd z_w mix_ready resid_var resid_rstd ln_done ffn_silu down_units "
    "od_rope od_gate ret_var ret_rstd ret_y route_in route_exp rank_in over_ready p_ready e_silu w_hi w_lo "
    "piece_used act_hi tok_hi back_zero out_done "
    "dve_step last_step"
).split()


def trunk(nc, x, c, positions, cond_w, cond_b, ln_w, ln_b, ev_w_in, ev_conv_w, ev_a_log, ev_dt_bias,
          ev_gdn_norm_w, ev_sinks, ev_w_out, ffn_w_up, ffn_w_down, od_w_in, od_gn_w, od_w_out,
          moe_w_router, moe_b_router, moe_w_up, moe_w_down, consts, out):
    fills, fills_before = psum_plan(pe_order())
    item_at, item_uses = item_plan()
    widths = {k: v.shape[1] for k, v in constant_table().items()}
    early = [k for k in widths if k not in LATE]
    N_RING = sum(widths[k] for k in early)
    CONST_COLS = sum(widths.values())

    with ExitStack() as ctx:
        def sb(name, shape, dt=F32):
            return ctx.enter_context(nc.sbuf_tensor(name, shape, dt))

        S = {n: ctx.enter_context(nc.semaphore(n)) for n in SEMS}
        weights_in = [ctx.enter_context(nc.semaphore(f"weights_in{i}")) for i in range(RING)]
        bank_full = [ctx.enter_context(nc.semaphore(f"bank_full{i}")) for i in range(8)]
        bank_free = [ctx.enter_context(nc.semaphore(f"bank_free{i}")) for i in range(8)]
        banks = [ctx.enter_context(nc.psum_tensor(f"bank{i}", [P, 512], F32)) for i in range(8)]

        ring = sb("ring", [P, RING * UNIT])
        xs = sb("xs", [P, NT, D])
        hs = sb("hs", [P, NT, D])
        hT = sb("hT", [P, KC, SEQ])
        mod = sb("mod", [P, 6 * D])
        acc = sb("acc", [P, 2, 512])
        ln = sb("ln", [P, 2, D])
        cst = sb("cst", [P, N_RING])
        cpart, off = {}, 0
        for k in early:
            cpart[k] = cst[:, off:off + widths[k]]
            off += widths[k]
        ident, ones = cpart["ident"], cpart["ones"]
        small = sb("small", [P, 572])
        posi = sb("posi", [P, NT], I32)
        over_int = sb("over_int", [1, 4], I32)
        with nc.sbuf_tensor("lower", [P, 4 * UNIT], F32) as lower, nc.sbuf_tensor("upper", [P, 6912], F32) as upper:
            pass
        w_hi, w_lo = (sb(n, [P, 3, PIECE], F32R) for n in ("w_hi", "w_lo"))
        eT_hi, eT_lo = (sb(n, [P, FFE // P, P], F32R) for n in ("eT_hi", "eT_lo"))
        heT_hi, heT_lo = (sb(n, [P, KC, P], F32R) for n in ("heT_hi", "heT_lo"))
        e_rows = sb("e_rows", [P, 1664])

        def carver(region):
            at = [0]

            def take(*dims):
                n = int(np.prod(dims))
                a = region[:, at[0]:at[0] + n]
                at[0] += n
                assert at[0] <= region.shape[1], (at[0], region.shape)
                if len(dims) == 1:
                    return a
                names = "abcde"[:len(dims)]
                return a.rearrange(f"p ({' '.join(names)}) -> p {' '.join(names)}",
                                   **{n_: d for n_, d in zip(names, dims)})
            return take

        def over_all(a, n):
            return a.unsqueeze(1).broadcast_to([P, n, a.shape[-1]])

        def per_row(a, n):
            return a.unsqueeze(2).broadcast_to([P, a.shape[-1], n])

        low, up, tiny = carver(lower), carver(upper), carver(small)
        conv_flat = low(NF * 259)
        conv_x = conv_flat.rearrange("p (c t) -> p c t", c=NF)
        conv_y = low(NF, SEQ)
        norm = low(2048)
        g_rhs, b_rhs, eG, dec, kbT, kbg, kdec = (low(NTH, P) for _ in range(7))
        trig = low(2, NT, NFREQ)
        vb, qdT = up(NTH, P), up(NTH, P)
        amask = up(2048)
        att_qk = up(NT, SH + SKV, SD)
        att_flat = upper[:, 4096:5376]
        att_v, att_qT, att_kT = up(NT, SKV * SD), up(NT, SG, P), up(NT, P)
        th = lambda a: a.rearrange("p (n j) -> p n j", n=NTH)
        X, Y = th(norm[:, 0:1024]), th(norm[:, 1024:2048])
        amasks = [th(amask[:, 0:1024]), th(amask[:, 1024:2048])]
        AXs, U, wT, vn = b_rhs, g_rhs, kbT, amasks[0]
        conv_blocks = conv_y.rearrange("p c (t j) -> p (c t) j", t=NT)
        o_tok, o_sq, aD = conv_blocks[:, 0:8], conv_blocks[:, 8:16], conv_blocks[:, 16:24]
        kT = lambda t, h: conv_blocks[:, 2 * (GH + h) + t]
        qT = lambda t, h: conv_blocks[:, 2 * h + t]
        vT = lambda t, h: conv_blocks[:, 2 * (2 * GH + h) + t]
        om = hs
        by_tile = lambda lo, t: conv_y[:, lo:lo + GH, t * P:(t + 1) * P]
        zs = mod[:, 0:1024].rearrange("p (t n) -> p t n", t=NT)
        qkT = th(mod[:, 1024:2048])
        state = hT[:, :, :].rearrange("p k t -> p (k t)").rearrange("p (n h j) -> p n h j", n=4, h=GH)
        scores = conv_flat[:, 0:3072].rearrange("p (b h k) -> p b h k", b=3, h=SH)
        ln_flat = ln[:, :, :].rearrange("p a n -> p (a n)")
        pT = [r.rearrange("p (h q) -> p h q", h=SH)
              for r in (ln_flat[:, 0:1024], ln_flat[:, 1024:2048], att_flat[:, 0:1024])]
        ang_take = carver(amask)
        ang = [ang_take(NT, NFREQ) for _ in range(4)]
        sin_t, cos_t = trig[:, 0], trig[:, 1]
        rope_take = carver(norm)
        rope_tmp = [rope_take(NT, SH + SKV, SROT) for _ in range(4)]
        conv_rows = upper[0:CONV_W * NF, 128:256]
        c_row = upper[0:KC, 0:128]
        conv_w = tiny(48)
        ab_w = tiny(KC, 8)
        gdnw = tiny(P)
        bias_rows = tiny(P)
        cT, eps_n, eps_ln = tiny(KC), tiny(1), tiny(1)
        posf = tiny(NT)
        beta, g_tok, g_col, e_after, bg, e_col, ssq, rstd_o = (tiny(NTH) for _ in range(8))
        ab = att_flat[:, 0:0] if False else tiny(NT, 8)
        g_a, g_b, g_c, g_d = (tiny(NTH) for _ in range(4))
        alog, dtb = tiny(GH), tiny(GH)
        stats, aggr, rstd = tiny(NT, 2, 6), tiny(NT, 2), tiny(NT)
        sinks, mx3, sm3, mx, es = low(SH), low(3, SH), low(3, SH), low(NT, SH), low(NT, SH)

        low, up = carver(lower), carver(upper)
        ffT = low(FFN // P, SEQ)
        ff_s, ff_a = up(2, NT, 256), up(2, NT, 256)
        assert FFN // P * SEQ <= 5632

        low, up = carver(lower), carver(upper)
        yT, ret_d, gnw, r_v, r_g = low(RH * RV // P, SEQ), low(RH, 2 * P), low(RH, RV), low(2, NT, RV), low(2, NT, RV)
        r_tmp = [low(2, P) for _ in range(4)]
        r_qk, r_qT, r_s, r_y = up(NT, 2, RK), up(4, SEQ), up(3 * P), up(NT, RV)

        er, mt = carver(e_rows), carver(mod[:, 0:4096])
        e_s, e_a = er(2, 256), er(2, 256)
        p_tok, pw_tok = er(NT, P), er(NT, P)
        pwT = mod[:, 4096:4096 + SEQ].rearrange("p (t s) -> p t s", t=NT)
        ye = acc
        ysum = hT[:, :, :].rearrange("p k t -> p (k t)").rearrange("p (t n) -> p t n", t=NT)
        strict, iota = mt(P), mt(P)
        late = mod[:, 0:2 * P]
        rw, rb = mt(KC, NE), mt(NE)
        logit, eq1, eq2, key_, l2 = (mt(NT, NE) for _ in range(5))
        m1, m2, i1, i2, e12, w1, w2 = (mt(NT) for _ in range(7))
        table, pick = mt(6, 2 * NE), mt(6, 2 * NE)
        picked, code, hot, item_no, cnt, over, rank_o = (mt(6), mt(2 * NE), mt(2 * NE), mt(1), mt(NE), mt(NE), mt(NE))
        over_hot, over_id = mt(3, NE), mt(3)

        TWO_PARTS = ("ffn_up", "od_qk")
        units, landed, last_in, before = {}, [0] * RING, [None] * RING, {}
        for i, k in enumerate(stream_units()):
            landed[i % RING] += 32 if k[0] in TWO_PARTS else 16
            units[k] = (i % RING, landed[i % RING])
            before[k] = last_in[i % RING]
            last_in[i % RING] = k
        cond_order = [k for k in stream_units() if k[0] == "cond"]
        partial = [k for k in stream_units() if k[0] in ("ffn_down", "od_out") and (k[0], k[1] + 1) in units]

        def wait_read(eng, key):
            if key[0] == "cond":
                eng.wait_ge(S["cond_acc"], cond_order.index(key) + 1)
            elif key in partial:
                eng.wait_ge(S["down_units"], partial.index(key) + 1)
            else:
                b, n = fills[(*key, 1)] if (*key, 1) in fills else fills[(key[0], 1, 1)]
                eng.wait_ge(bank_full[b], n + 1)
        SLOT_USES = N_UNITS // RING
        assert SLOT_USES * RING == N_UNITS

        BLOCKS = ((0, 0), (1, 0), (1, 1))

        def weights(eng, *key):
            s, count = units[key]
            eng.wait_ge(weights_in[s], count)
            return s, ring[:, s * UNIT:(s + 1) * UNIT]

        def to_fill(pe, *key):
            b, n = fills[key]
            if n:
                pe.wait_ge(bank_free[b], n)
            return banks[b], bank_full[b]

        def filled(eng, *key):
            b, n = fills[key]
            eng.wait_ge(bank_full[b], n + 1)
            return banks[b], bank_free[b]

        def taken(eng, *key):
            b, n = fills[key]
            eng.wait_ge(bank_free[b], n + 1)

        def item_taken(eng, it, *key, ago=0):
            b, n = item_at[key]
            eng.wait_ge(bank_free[b], it * item_uses[b] + (fills_before[b] + n + 1 - ago * item_uses[b]))

        def item_to_fill(pe, it, *key):
            b, n = item_at[key]
            pe.wait_ge(bank_free[b], it * item_uses[b] + (fills_before[b] + n))
            return banks[b], bank_full[b]

        def item_filled(eng, it, *key, ago=0):
            b, n = item_at[key]
            eng.wait_ge(bank_full[b], it * item_uses[b] + (fills_before[b] + n + 1 - ago * item_uses[b]))
            return banks[b], bank_free[b]

        def slot_landed(eng, it, a):
            slot, n = a % RING, a // RING
            eng.wait_ge(weights_in[slot], it * (32 * SLOT_USES) + (landed[slot] + 32 * n + 32))
            return ring[:, slot * UNIT:(slot + 1) * UNIT]

        def split(eng, sem, it, n):
            eng.wait_ge(S[sem], it * (2 * N_UNITS) + n)

        def piece_read(eng, it, n):
            u, half = n // 2, n % 2
            if n < 0:
                item_filled(eng, it, "down", 1, ago=1)
            elif half == 0:
                eng.wait_ge(S["piece_used"], it * N_UNITS + (u + 1))
            elif u < N_UP:
                item_filled(eng, it, "up", u)
            elif u < N_UNITS - 1:
                eng.wait_ge(S["down_units"], it * (N_DOWN - 1) + (len(partial) + u - N_UP + 1))
            else:
                item_filled(eng, it, "down", 1)

        def over_loop(eng, body):
            eng.wait_ge(S["over_ready"], 1)
            count = eng.value_load(over_int[0:1, 3:4], min_val=0, max_val=MAX_OVER)
            with eng.Fori(NE, N_ITEMS) as it:
                with eng.If(it < count + NE):
                    body(it)
                eng.nop()

        block = ctx.enter_context(nc.Block())

        @block.sync
        def _(sp):
            def kpn(w, a, b):
                return w[:, a:b].rearrange("(k p) n -> p k n", p=P)

            def halves(w, i):
                half = w.shape[1] // 2
                return [kpn(w, a + 256 * i, a + 256 * i + 256) for a in (0, half)]

            def source(key):
                kind, i = key[0], key[-1]
                q0 = QKV + GH * GD + 2 * GH
                if kind == "cond":
                    return kpn(cond_w[key[1]], 512 * i, 512 * i + 512)
                if kind == "ev_in":
                    a = 512 * i if i < 4 else q0 + 512 * (i - 4)
                    return kpn(ev_w_in[0], a, min(a + 512, ev_w_in.shape[2]))
                if kind == "ev_out":
                    return kpn(ev_w_out[0], 512 * i, 512 * i + 512)
                if kind == "ffn_up":
                    return halves(ffn_w_up[0], i)
                if kind == "od_qk":
                    return halves(od_w_in[0, :, 0:2 * RH * RK], i)
                if kind in ("od_v", "od_g"):
                    a = 2 * RH * RK + (RH * RV if kind == "od_g" else 0) + RV * i
                    return kpn(od_w_in[0], a, a + 512)
                w = ffn_w_down[0] if kind == "ffn_down" else od_w_out[0]
                return w[512 * i:min(512 * i + 512, w.shape[0])].rearrange("(k p) n -> p k n", p=P)

            def load(s, views):
                to = ring[:, s * UNIT:(s + 1) * UNIT]
                if not isinstance(views, list):
                    views = [views]
                for i, view in enumerate(views):
                    if view.shape[2] == D:
                        part = to.rearrange("p (k n) -> p k n", n=D)[:, 0:view.shape[1]]
                    else:
                        part = to.rearrange("p (k n) -> p k n", k=KC)[:, :, 256 * i:256 * i + view.shape[2]]
                    sp.dma_start(part, view).then_inc(weights_in[s], 16)

            for key in stream_units():
                s, _ = units[key]
                if before[key]:
                    wait_read(sp, before[key])
                load(s, source(key))

            def expert_unit(e, u, a):
                slot = a % RING
                to = ring[:, slot * UNIT:(slot + 1) * UNIT]
                if u < N_UP:
                    w = moe_w_up[0, e].rearrange("(k p) n -> p k n", p=P)
                    load(slot, [w[:, :, c0 + 256 * u:c0 + 256 * u + 256] for c0 in (0, FFE)])
                else:
                    for half in range(2):
                        r = 512 * (u - N_UP) + 256 * half
                        sp.dma_start(to[:, half * PIECE:(half + 1) * PIECE].rearrange("p (k n) -> p k n", n=D),
                                     moe_w_down[0, e, r:r + 256].rearrange("(k p) n -> p k n", p=P)) \
                            .then_inc(weights_in[slot], 16)

            for a in range(RING):
                wait_read(sp, last_in[a])
                expert_unit(0, a, a)
            for a in range(RING, N_UNITS + 1):
                split(sp, "w_lo", 0, 2 * (a - RING) + 2)
                expert_unit(a // N_UNITS, a % N_UNITS, a)
            with sp.Fori(1, NE) as it:
                for a in range(1, N_UNITS + 1):
                    split(sp, "w_lo", it, 2 * (a - RING) + 2)
                    expert_unit(it if a < N_UNITS else (it + 1) % NE, a % N_UNITS, a)

            def over_item(it):
                e = sp.value_load(over_int[0:1, bass.ds(it - NE, 1)], min_val=0, max_val=NE - 1)
                for u in range(N_UNITS):
                    split(sp, "w_lo", it, 2 * (u + 1 - RING) + 2)
                    expert_unit(e, u, u + 1)

            over_loop(sp, over_item)
            for t in range(NT):
                sp.wait_ge(S["ln_done"], 3 * NT + t + 1)
                sp.dma_start(out[0, t * P:(t + 1) * P, :], xs[:, t]).then_inc(S["out_done"], 16)
            sp.wait_ge(S["out_done"], 16 * NT)

        @block.tensor
        def _(pe):
            mm = nc.tensor.matmul
            pe.wait_ge(S["consts_in"], 16)
            pe.wait_ge(S["c_act"], 1)
            bank, full = to_fill(pe, "cT")
            nc.tensor.transpose(bank[:, 0:KC], c_row, ident[0:KC, 0:KC]).then_inc(full, 1)
            pe.wait_ge(S["convw_in"], 16)
            bank, full = to_fill(pe, "convT")
            nc.tensor.transpose(bank[:, 0:48], conv_rows, ident[0:48, 0:48]).then_inc(full, 1)

            cond_n = [0]

            def cond(l, u):
                i = cond_n[0]
                cond_n[0] += 1
                bank, full = to_fill(pe, "cond", l, u)
                pe.wait_ge(S["cond_acc"], i + 1)
                mm(bank[:], ones, acc[:, i % 2], start=True, stop=True).then_inc(full, 1)

            def turn(stage, ready, per_tile):
                for i in range(4):
                    t, half = i // 2, i % 2
                    pe.wait_ge(S[ready], per_tile[t])
                    bank, full = to_fill(pe, "hT", stage, i)
                    for j in range(4):
                        k = 4 * half + j
                        last = nc.tensor.transpose(bank[:, j * P:(j + 1) * P], hs[:, t, k * P:(k + 1) * P], ident)
                    last.then_inc(full, 1)

            def project(key, stage, n=512):
                _, w = weights(pe, *key)
                w = w.rearrange("p (k n) -> p k n", k=KC)
                for t in range(NT):
                    taken(pe, "hT", stage, 2 * t + 1)
                    bank, full = to_fill(pe, *key, t)
                    for k in range(KC):
                        last = mm(bank[:, 0:n], hT[:, k, t * P:(t + 1) * P], w[:, k, 0:n],
                                  start=(k == 0), stop=(k == KC - 1))
                    last.then_inc(full, 1)

            for u in range(4):
                cond(0, u)
            turn(0, "h_ready", (1, 2))
            pe.wait_ge(S["abw_in"], 16)
            for t in range(NT):
                taken(pe, "hT", 0, 2 * t + 1)
                bank, full = to_fill(pe, "ab", t)
                for k in range(KC):
                    last = mm(bank[:, 0:8], hT[:, k, t * P:(t + 1) * P], ab_w[:, k], start=(k == 0), stop=(k == KC - 1))
                last.then_inc(full, 1)
            for u, c_ in ((0, 4), (1, 5), (2, None)):
                _, w = weights(pe, "ev_in", u)
                w = w.rearrange("p (k n) -> p k n", k=KC)
                taken(pe, "hT", 0, 3)
                for i in range(2):
                    bank, full = to_fill(pe, "ev_in", u, i)
                    for j in range(2):
                        f = (2 * i + j) * P
                        for k in range(KC):
                            last = mm(bank[:, j * SEQ:(j + 1) * SEQ], w[:, k, f:f + P], hT[:, k],
                                      start=(k == 0), stop=(k == KC - 1))
                    last.then_inc(full, 1)
                if c_:
                    cond(0, c_)
            project(("ev_in", 5), 0, 256)
            project(("ev_in", 4), 0)
            cond(0, 6)
            project(("ev_in", 3), 0)
            pe.wait_ge(S["squared"], 1)
            for i in range(4):
                bank, full = to_fill(pe, "l2", i)
                mm(bank[:], ones, norm[:, 512 * i:512 * i + 512], start=True, stop=True).then_inc(full, 1)
            pe.wait_ge(S["g_rhs"], 1)
            for t in range(NT):
                bank, full = to_fill(pe, "g_row", t)
                mm(bank[:], ones, g_rhs[:, GH * t:GH * t + GH], start=True, stop=True).then_inc(full, 1)
            pe.wait_ge(S["b_rhs"], 1)
            for t in range(NT):
                bank, full = to_fill(pe, "b_row", t)
                mm(bank[:], ones, b_rhs[:, GH * t:GH * t + GH], start=True, stop=True).then_inc(full, 1)
            bank, full = to_fill(pe, "g_after")
            mm(bank[:, 0:NTH], cpart["after"], g_tok, start=True, stop=True).then_inc(full, 1)
            pe.wait_ge(S["qk_norm"], 4)
            for name, block_of, ready in (("k_tok", kT, "k_act"), ("v_tok", vT, "v_act")):
                pe.wait_ge(S[ready], 1)
                for t in range(NT):
                    bank, full = to_fill(pe, name, t)
                    for h in range(GH):
                        last = nc.tensor.transpose(bank[:, h * P:(h + 1) * P], block_of(t, h), ident)
                    last.then_inc(full, 1)
            for name, other in (("kk", lambda t, h: kbT[:, GH * t + h]), ("qk", qT)):
                for t in range(NT):
                    if name == "kk":
                        taken(pe, "b_row", t)
                    bank, full = to_fill(pe, name, t)
                    for h in range(GH):
                        last = mm(bank[:, h * P:(h + 1) * P], kT(t, h), other(t, h), start=True, stop=True)
                    last.then_inc(full, 1)
            for t in range(NT):
                pe.wait_ge(S["y0_ready"], t + 1)
                bank, full = to_fill(pe, "xt", t)
                for h in range(GH):
                    last = nc.tensor.transpose(bank[:, h * P:(h + 1) * P], Y[:, GH * t + h], ident)
                last.then_inc(full, 1)
            pe.wait_ge(S["rope_done"], 2)
            for t in range(NT):
                bank, full = to_fill(pe, "att_T", t)
                for g in range(SG):
                    last = nc.tensor.transpose(
                        bank[:, g * P:(g + 1) * P],
                        att_qk[:, t, 2 * g:2 * g + 2].rearrange("p h d -> p (h d)"), ident)
                last.then_inc(full, 1)
            bank, full = to_fill(pe, "att_T", 2)
            for t in range(NT):
                last = nc.tensor.transpose(
                    bank[:, t * P:(t + 1) * P], att_qk[:, t, SH:SH + SKV].rearrange("p h d -> p (h d)"), ident)
            last.then_inc(full, 1)
            for i in range(3):
                taken(pe, "att_T", i)
            for b, (tq, tk) in enumerate(BLOCKS):
                for v in range(SKV):
                    bank, full = to_fill(pe, "score", b, v)
                    rows = slice(SD * v, SD * v + SD)
                    for g in range(SG):
                        last = mm(bank[:, g * P:(g + 1) * P], att_qT[rows, tq, g], att_kT[rows, tk],
                                  start=True, stop=True)
                    last.then_inc(full, 1)

            def products(key, lhs, rhs):
                bank, full = to_fill(pe, *key)
                t = key[-1]
                for h in range(GH):
                    n = GH * t + h
                    last = mm(bank[:, h * P:(h + 1) * P], lhs[:, n], rhs[:, n], start=True, stop=True)
                last.then_inc(full, 1)

            for l in range(1, N_LEVELS):
                for t in range(NT):
                    pe.wait_ge(S["level_mask"], 2 * l + t + 1)
                    if l == 1:
                        taken(pe, "xt", t)
                    else:
                        taken(pe, "xax", l - 1, t)
                    products(("ax", l, t), amasks[l % 2], X)
                for name in ("xax", "yay") if l < N_LEVELS - 1 else ("yay",):
                    for t in range(NT):
                        taken(pe, "ax", l, t)
                        if l > 1:
                            taken(pe, "yay", l - 1, t)
                        products((name, l, t), *((Y, AXs) if name == "xax" else (AXs, Y)))
                cond(0, 6 + l)
            for t in range(NT):
                taken(pe, "v_tok", t)
                taken(pe, "yay", N_LEVELS - 1, t)
                products(("u", t), Y, vb)
            for t in range(NT):
                taken(pe, "k_tok", t)
                products(("w", t), kbg, Y)
            for b in range(3):
                pe.wait_ge(S["prob_exp"], b + 1)
                for v in range(SKV):
                    bank, full = to_fill(pe, "prob_T", b, v)
                    for g in range(SG):
                        last = nc.tensor.transpose(bank[:, g * P:(g + 1) * P], scores[:, b, SG * v + g], ident)
                    last.then_inc(full, 1)
            for t in range(NT):
                mine = [b for b, (tq, _) in enumerate(BLOCKS) if tq == t]
                for b in mine:
                    for v in range(SKV):
                        taken(pe, "prob_T", b, v)
                bank, full = to_fill(pe, "pv", t)
                for h in range(SH):
                    for b in mine:
                        last = mm(bank[:, h * SD:(h + 1) * SD], pT[b][:, h],
                                  att_v[:, BLOCKS[b][1], (h // SG) * SD:(h // SG + 1) * SD],
                                  start=(b == mine[0]), stop=(b == mine[-1]))
                last.then_inc(full, 1)
            def v_ready(eng, n):
                if n:
                    taken(eng, "ws", n)
                else:
                    eng.wait_ge(S["v_first"], 1)

            for n in range(4):
                t, rows = n // 2, slice(CHUNK * (n % 2), CHUNK * (n % 2) + CHUNK)
                if n:
                    taken(pe, "w", t)
                    taken(pe, "kv", n - 1)
                    bank, full = to_fill(pe, "ws", n)
                    for h in range(GH):
                        last = mm(bank[:, h * P:(h + 1) * P], wT[:, GH * t + h], state[:, n, h], start=True, stop=True)
                    last.then_inc(full, 1)
                if n < 3:
                    v_ready(pe, n)
                    bank, full = to_fill(pe, "kv", n)
                    for h in range(GH):
                        last = mm(bank[:, h * P:(h + 1) * P], kdec[rows, GH * t + h], vn[rows, GH * t + h],
                                  start=True, stop=True)
                    last.then_inc(full, 1)
            pe.wait_ge(S["q_dec"], 2)
            for t in range(NT):
                v_ready(pe, 2 * t + 1)
                taken(pe, "kv", 2 * t)
                taken(pe, "qk", t)
                bank, full = to_fill(pe, "go", t)
                for h in range(GH):
                    for c_ in range(2):
                        n, rows = 2 * t + c_, slice(CHUNK * c_, CHUNK * c_ + CHUNK)
                        if n:
                            mm(bank[rows, h * P:(h + 1) * P], qdT[:, GH * t + h, rows], state[:, n, h],
                               start=True, stop=False)
                        last = mm(bank[rows, h * P:(h + 1) * P], qkT[:, GH * t + h, rows], vn[:, GH * t + h],
                                  start=not n, stop=True)
                last.then_inc(full, 1)
            turn(1, "mix_ready", (1, 2))
            project(("ev_out", 0), 1)
            project(("ev_out", 1), 1)
            turn(2, "h_ready", (3, 4))

            def down(kind, lhs, n_units, n_chunks):
                outs = {(t, h): to_fill(pe, kind, t, h) for t in range(NT) for h in range(2)}
                for i in range(n_units):
                    _, w = weights(pe, kind, i)
                    w = w.rearrange("p (k n) -> p k n", n=D)
                    k_n = min(4, n_chunks - 4 * i)
                    for (t, h), (bank, full) in outs.items():
                        for k in range(k_n):
                            ch = 4 * i + k
                            last = mm(bank[:], lhs[:, ch, t * P:(t + 1) * P], w[:, k, h * 512:(h + 1) * 512],
                                      start=(ch == 0), stop=(ch == n_chunks - 1))
                        if i == n_units - 1:
                            last.then_inc(full, 1)
                    if i < n_units - 1:
                        last.then_inc(S["down_units"], 1)

            def ffn_turn(u):
                for t in range(NT):
                    taken(pe, "ffn_up", u, t)
                bank, full = to_fill(pe, "ffn_T", u)
                for j in range(2):
                    for t in range(NT):
                        last = nc.tensor.transpose(bank[:, (2 * j + t) * P:(2 * j + t + 1) * P],
                                                   ff_a[:, u % 2, t, j * P:(j + 1) * P], ident)
                last.then_inc(full, 1)

            for u in range(FFN // 256):
                project(("ffn_up", u), 2)
                if 1 <= u <= 10:
                    cond(1, u - 1)
                if u:
                    ffn_turn(u - 1)
            ffn_turn(FFN // 256 - 1)
            for u in range(FFN // 256):
                taken(pe, "ffn_T", u)
            down("ffn_down", ffT, 6, FFN // P)
            turn(3, "h_ready", (5, 6))
            cond(1, 10)
            cond(1, 11)
            for h in range(RH + 1):
                if h < RH:
                    project(("od_qk", h), 3)
                if h:
                    g = h - 1
                    taken(pe, "ret_s", g)
                    for t in range(NT):
                        taken(pe, "od_v", g, t)
                    for t in range(NT):
                        bank, full = to_fill(pe, "ret_y", g, t)
                        for j in range(t + 1):
                            b0 = (0, P, 2 * P)[t + j]
                            last = mm(bank[:], r_s[:, b0:b0 + P], r_v[:, g % 2, j], start=(j == 0), stop=(j == t))
                        last.then_inc(full, 1)
                if h < RH:
                    project(("od_v", h), 3)
                    for t in range(NT):
                        pe.wait_ge(S["od_rope"], 2 * h + t + 1)
                        bank, full = to_fill(pe, "ret_T", h, t)
                        for a in range(4):
                            last = nc.tensor.transpose(bank[:, a * P:(a + 1) * P],
                                                       r_qk[:, t, a // 2, (a % 2) * P:(a % 2 + 1) * P], ident)
                        last.then_inc(full, 1)
                    project(("od_g", h), 3)
                    for t in range(NT):
                        taken(pe, "ret_T", h, t)
                    bank, full = to_fill(pe, "ret_s", h)
                    for j, q0 in ((0, 0), (1, P)):
                        for a in range(2):
                            last = mm(bank[:, j * SEQ:j * SEQ + SEQ - q0], r_qT[:, 2 + a, j * P:(j + 1) * P],
                                      r_qT[:, a, q0:SEQ], start=(a == 0), stop=(a == 1))
                    last.then_inc(full, 1)
                if h:
                    for t in range(NT):
                        pe.wait_ge(S["ret_y"], 2 * g + t + 1)
                        bank, full = to_fill(pe, "ret_yT", g, t)
                        for a in range(4):
                            last = nc.tensor.transpose(bank[:, a * P:(a + 1) * P], r_y[:, t, a * P:(a + 1) * P], ident)
                        last.then_inc(full, 1)
            for h in range(RH):
                for t in range(NT):
                    taken(pe, "ret_yT", h, t)
            down("od_out", yT, 4, RH * RV // P)
            turn(4, "h_ready", (7, 8))
            pe.wait_ge(S["router_in"], 32)
            for i in range(4):
                taken(pe, "hT", 4, i)
            bank, full = to_fill(pe, "router")
            for t in range(NT):
                for k in range(KC):
                    last = mm(bank[:, t * NE:(t + 1) * NE], hT[:, k, t * P:(t + 1) * P], rw[:, k],
                              start=(k == 0), stop=(k == KC - 1))
            last.then_inc(full, 1)
            pe.wait_ge(S["late_in"], 16)
            pe.wait_ge(S["rank_in"], 1)
            bank, full = to_fill(pe, "rank")
            mask = [table[:, 2 + t, 0:NE] for t in range(NT)]
            mm(bank[:, 0:NE], strict, mask[0], start=True, stop=True)
            mm(bank[:, NE:2 * NE], strict, mask[1], start=True, stop=False)
            mm(bank[:, NE:2 * NE], ones, mask[0], start=False, stop=True)
            mm(bank[:, 2 * NE:3 * NE], ones, mask[0], start=True, stop=False)
            mm(bank[:, 2 * NE:3 * NE], ones, mask[1], start=False, stop=True).then_inc(full, 1)

            def gather(fill):
                for half in range(2):
                    bank, full = fill(half)
                    for j in range(4):
                        k = 4 * half + j
                        for t in range(NT):
                            last = mm(bank[:, j * P:(j + 1) * P], hs[:, t, k * P:(k + 1) * P], p_tok[:, t],
                                      start=(t == 0), stop=(t == NT - 1))
                    last.then_inc(full, 1)

            pe.wait_ge(S["p_ready"], 1)
            gather(lambda half: to_fill(pe, "gather", half))

            def three(bank, lhs, rhs, start, stop):
                mm(bank, lhs[0], rhs[1], start=start, stop=False)
                mm(bank, lhs[1], rhs[0], start=False, stop=False)
                return mm(bank, lhs[0], rhs[0], start=False, stop=stop)

            def back(it):
                for h in range(2):
                    item_taken(pe, it, "down", h, ago=1)
                for i in range(4):
                    bank, full = item_to_fill(pe, it, "back", i)
                    mm(bank[:], pwT[:, i // 2], ye[:, i % 2], start=True, stop=True).then_inc(full, 1)

            def item(it, late=0):
                def act_turn(u):
                    item_taken(pe, it, "up", u)
                    bank, full = item_to_fill(pe, it, "act_T", u)
                    for j in range(2):
                        last = nc.tensor.transpose(bank[:, j * P:(j + 1) * P], e_a[:, u % 2, j * P:(j + 1) * P], ident)
                    last.then_inc(full, 1)

                def piece(u, half, view):
                    n = 2 * (u + late) + half
                    split(pe, "w_lo", it, n + 1)
                    return [view(a[:, n % 3]) for a in (w_hi, w_lo)]

                for u in range(N_UP):
                    bank, full = item_to_fill(pe, it, "up", u)
                    for half in range(2):
                        w = piece(u, half, lambda a: a.rearrange("p (k n) -> p k n", k=KC // 2))
                        for k in range(KC // 2):
                            kk = KC // 2 * half + k
                            last = three(bank[:], (heT_hi[:, kk], heT_lo[:, kk]), [a[:, k] for a in w],
                                         kk == 0, kk == KC - 1)
                        last.then_inc(full if half else S["piece_used"], 1)
                        if half == 0 and u:
                            act_turn(u - 1)
                    if u == 0:
                        back(it)
                        pe.wait_ge(S["p_ready"], it + 1)
                        bank, full = item_to_fill(pe, it, "pwT")
                        for t in range(NT):
                            last = nc.tensor.transpose(bank[:, t * P:(t + 1) * P], pw_tok[:, t], ident)
                        last.then_inc(full, 1)
                outs = [item_to_fill(pe, it, "down", h) for h in range(2)]
                for i in range(N_DOWN):
                    for u in (2 * i, 2 * i + 1):
                        item_taken(pe, it, "act_T", u)
                    for half in range(2):
                        w = piece(N_UP + i, half, lambda a: a.rearrange("p (k n) -> p k n", n=D))
                        for h, (bank, full) in enumerate(outs):
                            for k in range(2):
                                ch = 4 * i + 2 * half + k
                                last = three(bank[:], (eT_hi[:, ch], eT_lo[:, ch]),
                                             [a[:, k, h * 512:(h + 1) * 512] for a in w],
                                             ch == 0, ch == 4 * N_DOWN - 1)
                            if half and i == N_DOWN - 1:
                                last.then_inc(full, 1)
                        if half == 0:
                            last.then_inc(S["piece_used"], 1)
                            if i == 0:
                                act_turn(N_UP - 1)
                            if i == 1:
                                pe.wait_ge(S["p_ready"], it + 2)
                                gather(lambda part: item_to_fill(pe, it, "gather", part))
                        elif i < N_DOWN - 1:
                            last.then_inc(S["down_units"], 1)
                for half in range(2):
                    item_taken(pe, it, "gather", half)

            for half in range(2):
                taken(pe, "gather", half)
            pe.wait_ge(S["back_zero"], 2)
            with pe.Fori(0, NE) as it:
                item(it)
            over_loop(pe, lambda it: item(it, 1))
            pe.wait_ge(S["over_ready"], 1)
            back(pe.value_load(over_int[0:1, 3:4], min_val=0, max_val=MAX_OVER) + NE)

        @block.scalar
        def _(act):
            f = nc.scalar.activation
            act.dma_start(c_row, c[0].rearrange("(k p) -> k p", p=P)).then_inc(S["c_in"], 16)
            act.dma_start(posi[:], positions[0].rearrange("(t p) -> p t", p=P),
                          allow_slow_non_contiguous=True).then_inc(S["c_in"], 16)
            act.dma_start(cst[:], consts[:, 0:N_RING]).then_inc(S["consts_in"], 16)
            act.dma_start(xs[:], x[0].rearrange("(t p) d -> p t d", p=P)).then_inc(S["x_in"], 16)
            act.dma_start(bias_rows[0:96], cond_b.rearrange("l (r q) -> (l r) q", q=P)).then_inc(S["bias_in"], 16)
            act.dma_start(conv_rows, ev_conv_w[0].rearrange("j (c p) -> (j c) p", p=P)).then_inc(S["convw_in"], 16)
            act.dma_start(ab_w, ev_w_in[0, :, QKV + GH * GD:QKV + GH * GD + 2 * GH]
                          .rearrange("(k p) n -> p k n", p=P)).then_inc(S["abw_in"], 16)
            act.wait_ge(S["c_in"], 32)
            f(c_row, c_row, ACT.Silu).then_inc(S["c_act"], 1)

            def cond(l, u):
                if l == 1:
                    if u < 10:
                        act.wait_ge(S["h_ready"], 4)
                    else:
                        act.wait_ge(S["ln_done"], 4)
                bank, free = filled(act, "cond", l, u)
                scale = 1.0 if u // 2 in (1, 4) else 0.0
                f(mod[:, 512 * u:512 * u + 512], bank[:], ACT.Copy, bias=scale).then_inc(free, 1)

            def copy(key, to, view=None, func=ACT.Copy, scale=1.0):
                bank, free = filled(act, *key)
                src = bank[:] if view is None else view(bank)
                f(to, src, func, scale=scale).then_inc(free, 1)

            def turned(stage):
                for i in range(4):
                    t, half = i // 2, i % 2
                    copy(("hT", stage, i), hT[:, 4 * half:4 * half + 4, t * P:(t + 1) * P],
                         lambda b: b[:].rearrange("p (k s) -> p k s", k=4))

            heads = lambda b: b[:].rearrange("p (h j) -> p h j", h=GH)

            for i in range(2):
                act.wait_ge(S["angle_ready"], i + 1)
                f(trig[:, i], ang[i], ACT.Sin).then_inc(S["trig_ready"], 1)
            for u in range(4):
                cond(0, u)
            turned(0)
            for t in range(NT):
                copy(("ab", t), ab[:, t], lambda b: b[:, 0:8])
            act.wait_ge(S["pads_zero"], 1)
            for u, c_ in ((0, 4), (1, 5), (2, None)):
                for i in range(2):
                    c0 = 4 * u + 2 * i
                    copy(("ev_in", u, i), conv_x[:, c0:c0 + 2, CONV_W - 1:],
                         lambda b: b[:].rearrange("p (c t) -> p c t", c=2))
                if c_:
                    cond(0, c_)
            for t in range(NT):
                bank, free = filled(act, "ev_in", 5, t)
                f(att_qk[:, t, SH:], bank[:, 0:P].rearrange("p (h d) -> p h d", h=SKV), ACT.Copy).then_inc(S["k_raw"], 1)
                f(att_v[:, t], bank[:, P:2 * P], ACT.Copy).then_inc(free, 1)
            for t in range(NT):
                copy(("ev_in", 4, t), att_qk[:, t, 0:SH].rearrange("p (g v) d -> p g v d", v=SKV),
                     lambda b: b[:].rearrange("p (v g d) -> p g v d", v=SKV, g=SG))
            act.wait_ge(S["gates_in"], 32)
            act.wait_ge(S["gate_in"], 2)
            f(g_a, g_a, ACT.Exp, scale=-1.0).then_inc(S["gate_exp"], 1)
            f(g_b, g_b, ACT.Exp).then_inc(S["gate_exp"], 1)
            f(alog, alog, ACT.Exp).then_inc(S["gate_exp"], 1)
            cond(0, 6)
            act.wait_ge(S["h_ready"], 2)
            for t in range(NT):
                copy(("ev_in", 3, t), zs[:, t], func=ACT.Silu)
            for name, lo in (("q_act", 0), ("k_act", GH), ("v_act", 2 * GH)):
                act.wait_ge(S["conv_done"], lo // GH + 1)
                f(conv_y[:, lo:lo + GH], conv_y[:, lo:lo + GH], ACT.Silu).then_inc(S[name], 1)
            for i, name in enumerate(("q_act", "k_act")):
                act.wait_ge(S[name], 1)
                last = f(norm[:, 1024 * i:1024 * i + 1024].rearrange("p (c t) -> p c t", c=GH),
                         conv_y[:, GH * i:GH * i + GH], ACT.Square)
            last.then_inc(S["squared"], 1)
            for i in range(4):
                bank, free = filled(act, "l2", i)
                f(norm[:, 512 * i:512 * i + 512], bank[:], ACT.Sqrt, bias=eps_n).then_inc(free, 1)
            for t in range(NT):
                bank, _ = filled(act, "g_row", t)
                f(eG[:, GH * t:GH * t + GH], heads(bank), ACT.Exp).then_inc(S["exp_row"], 1)
            copy(("g_after",), e_after, lambda b: b[:, 0:NTH], ACT.Exp)
            for t in range(NT):
                taken(act, "g_row", t)
                f(dec[:, GH * t:GH * t + GH], dec[:, GH * t:GH * t + GH], ACT.Exp).then_inc(S["dec_exp"], 1)
            f(e_col, g_col, ACT.Exp).then_inc(S["e_col"], 1)
            for t in range(NT):
                copy(("xt", t), X[:, GH * t:GH * t + GH], heads)
            for t in range(NT):
                copy(("att_T", t), att_qT[:, t], heads)
            copy(("att_T", 2), att_kT, lambda b: b[:, 0:NT * P].rearrange("p (t j) -> p t j", t=NT))
            for l in range(1, N_LEVELS):
                for t in range(NT):
                    copy(("ax", l, t), AXs[:, GH * t:GH * t + GH], heads)
                if 2 <= l < 5:
                    b = l - 2
                    act.wait_ge(S["score_sub"], b + 1)
                    f(scores[:, b], scores[:, b], ACT.Exp).then_inc(S["prob_exp"], 1)
                cond(0, 6 + l)
            act.wait_ge(S["sink_sub"], 1)
            f(es, es, ACT.Exp).then_inc(S["sink_exp"], 1)
            for t in range(NT):
                copy(("u", t), U[:, GH * t:GH * t + GH], heads)
            for t in range(NT):
                copy(("w", t), wT[:, GH * t:GH * t + GH], heads)
            for b in range(3):
                for v in range(SKV):
                    copy(("prob_T", b, v), pT[b][:, SG * v:SG * v + SG], heads)
            for t in range(NT):
                copy(("go", t), o_tok[:, GH * t:GH * t + GH], heads)
            for t in range(NT):
                act.wait_ge(S["ssq_ready"], t + 1)
                f(rstd_o[:, GH * t:GH * t + GH], ssq[:, GH * t:GH * t + GH], ACT.Sqrt, bias=eps_n,
                  scale=1.0 / GD).then_inc(S["o_rstd"], 1)

            def deviations(var_ready, done, first, eps):
                for t in range(NT):
                    act.wait_ge(S[var_ready], first + t + 1)
                    f(rstd[:, t:t + 1], aggr[:, t, 1:2], ACT.Sqrt, bias=eps).then_inc(S[done], 1)

            turned(1)
            deviations("resid_var", "resid_rstd", 0, eps_ln)
            turned(2)
            for u in range(FFN // 256):
                for t in range(NT):
                    if u >= 2:
                        taken(act, "ffn_up", u - 2, t)
                    bank, _ = filled(act, "ffn_up", u, t)
                    f(ff_s[:, u % 2, t], bank[:, 0:256], ACT.Silu).then_inc(S["ffn_silu"], 1)
                if 1 <= u <= 10:
                    cond(1, u - 1)
                if u:
                    copy(("ffn_T", u - 1), ffT[:, 2 * u - 2:2 * u], lambda b: b[:].rearrange("p (j s) -> p j s", j=2))
            copy(("ffn_T", FFN // 256 - 1), ffT[:, FFN // P - 2:], lambda b: b[:].rearrange("p (j s) -> p j s", j=2))
            deviations("resid_var", "resid_rstd", NT, eps_ln)
            turned(3)
            cond(1, 10)
            cond(1, 11)
            for h in range(RH + 1):
                if h:
                    deviations("ret_var", "ret_rstd", NT * (h - 1), eps_n)
                if h < RH:
                    for t in range(NT):
                        if h >= 2:
                            filled(act, "ret_y", h - 2, NT - 1)
                        copy(("od_v", h, t), r_v[:, h % 2, t])
                    for t in range(NT):
                        copy(("ret_T", h, t), r_qT[:, :, t * P:(t + 1) * P], heads)
                    for t in range(NT):
                        if h >= 2:
                            act.wait_ge(S["ret_y"], 2 * (h - 2) + NT)
                        copy(("od_g", h, t), r_g[:, h % 2, t], func=ACT.Silu)
                if h:
                    for t in range(NT):
                        copy(("ret_yT", h - 1, t), yT[:, 4 * (h - 1):4 * h, t * P:(t + 1) * P], heads)
            deviations("resid_var", "resid_rstd", 2 * NT, eps_ln)
            turned(4)
            act.wait_ge(S["route_in"], 1)
            f(e12, e12, ACT.Exp).then_inc(S["route_exp"], 1)
            for half in range(2):
                bank, _ = filled(act, "gather", half)
                f(heT_hi[:, 4 * half:4 * half + 4], heads(bank), ACT.Copy).then_inc(S["tok_hi"], 1)

            def item(it, late=0):
                def take(key, to, view, func=ACT.Copy):
                    bank, free = item_filled(act, it, *key)
                    f(to, view(bank), func).then_inc(free, 1)

                def split_unit(u):
                    w = slot_landed(act, it, u + late)
                    for half in range(2):
                        n = 2 * u + half
                        piece_read(act, it, n - 3)
                        f(w_hi[:, (n + 2 * late) % 3], w[:, half * PIECE:(half + 1) * PIECE], ACT.Copy) \
                            .then_inc(S["w_hi"], 1)

                if late:
                    split(act, "w_lo", it, 2)
                    split_unit(0)
                for u in range(N_UNITS):
                    if 1 <= u <= N_UP:
                        item_taken(act, it, "up", (u - 3) % N_UP, ago=int(u < 3))
                        bank, _ = item_filled(act, it, "up", u - 1)
                        f(e_s[:, (u - 1) % 2], bank[:, 0:256], ACT.Silu).then_inc(S["e_silu"], 1)
                    if u < N_UNITS - late:
                        split_unit(u + 1)
                    if u == 0:
                        take(("pwT",), pwT, lambda b: b[:, 0:SEQ].rearrange("p (t s) -> p t s", t=NT))
                    if 1 <= u <= N_UP:
                        bank, _ = item_filled(act, it, "act_T", u - 1)
                        f(eT_hi[:, 2 * u - 2:2 * u], bank[:, 0:256].rearrange("p (j s) -> p j s", j=2),
                          ACT.Copy).then_inc(S["act_hi"], 1)
                    if u == N_UP + 1:
                        for half in range(2):
                            bank, _ = item_filled(act, it, "gather", half)
                            f(heT_hi[:, 4 * half:4 * half + 4], heads(bank), ACT.Copy).then_inc(S["tok_hi"], 1)
                for h in range(2):
                    take(("down", h), ye[:, h], lambda b: b[:])

            w = slot_landed(act, 0, 0)
            for half in range(2):
                f(w_hi[:, half], w[:, half * PIECE:(half + 1) * PIECE], ACT.Copy).then_inc(S["w_hi"], 1)
            with act.Fori(0, NE) as it:
                item(it)
            over_loop(act, lambda it: item(it, 1))
            deviations("resid_var", "resid_rstd", 3 * NT, eps_ln)

        @block.vector
        def _(dve):
            V = Steps(dve, S["dve_step"])
            tt, ts, stt = nc.vector.tensor_tensor, nc.vector.tensor_scalar, nc.vector.scalar_tensor_tensor
            quad = lambda a, t: a[:, GH * t:GH * t + GH]
            heads = lambda b: b[:].rearrange("p (h j) -> p h j", h=GH)

            V.do(nc.vector.memset(eps_n, NORM_EPS))
            V.do(nc.vector.memset(eps_ln, LN_EPS))
            nc.vector.memset(conv_x[:, :, 0:CONV_W - 1], 0.0).then_inc(S["pads_zero"], 1)
            bank, free = filled(dve, "cT")
            nc.vector.tensor_copy(cT, bank[:, 0:KC]).then_inc(free, 1)
            bank, free = filled(dve, "convT")
            nc.vector.tensor_copy(conv_w, bank[:, 0:48]).then_inc(free, 1)
            dve.wait_ge(S["consts_in"], 16)
            dve.wait_ge(S["c_in"], 32)
            V.then(nc.vector.tensor_copy(posf, posi[:]))
            for t in range(NT):
                V.do(ts(ang[2][:, t], cpart["freq"], posf[:, t:t + 1], None, ALU.mult))
            V.wait()
            V.then(ts(ang[3], ang[2], 1.0 / TWO_PI, ROUND, ALU.mult, ALU.add))
            V.then(ts(ang[3], ang[3], ROUND, None, ALU.subtract))
            for part in (PI2_A, PI2_B, PI2_C):
                V.then(stt(ang[2], ang[3], -part, ang[2], ALU.mult, ALU.add))
            ts(ang[0], ang[2], PI_MAX, -PI_MAX, ALU.min, ALU.max).then_inc(S["angle_ready"], 1)
            V.then(ts(ang[2], ang[2], TWO_PI / 4, None, ALU.add))
            V.then(ts(ang[3], ang[2], PI_MAX, -TWO_PI, ALU.is_gt, ALU.mult))
            V.then(tt(ang[2], ang[2], ang[3], ALU.add))
            ts(ang[1], ang[2], PI_MAX, -PI_MAX, ALU.min, ALU.max).then_inc(S["angle_ready"], 1)

            cond_n = [0]
            dve.wait_ge(S["bias_in"], 16)
            taken(dve, "cT")

            def cond(l, u):
                i = cond_n[0]
                cond_n[0] += 1
                to = acc[:, i % 2]
                if i >= 2:
                    filled(dve, *cond_order[i - 2])
                _, w = weights(dve, "cond", l, u)
                w = w.rearrange("p (k n) -> p k n", k=KC)
                V.then(ts(to, w[:, 0], cT[:, 0:1], None, ALU.mult))
                for k in range(1, KC):
                    V.then(stt(to, w[:, k], cT[:, k:k + 1], to, ALU.mult, ALU.add))
                for j in range(4):
                    row = 48 * l + 4 * u + j
                    cols = slice(j * P, (j + 1) * P)
                    last = stt(to[0:96, cols], bias_rows[0:96], ident[0:96, row:row + 1], to[0:96, cols], ALU.mult, ALU.add)
                    if j < 3:
                        V.do(last)
                last.then_inc(S["cond_acc"], 1)

            def modulate(l, shift):
                a = shift * D
                for u in range(2 * shift, 2 * shift + 4):
                    taken(dve, "cond", l, u)
                for t in range(NT):
                    V.then(tt(hs[:, t], xs[:, t], mod[:, a + D:a + 2 * D], ALU.mult))
                    tt(hs[:, t], hs[:, t], mod[:, a:a + D], ALU.add).then_inc(S["h_ready"], 1)

            def residual(l, gate, key, t, half):
                cols = slice(512 * half, 512 * half + 512)
                for u in (2 * gate, 2 * gate + 1):
                    taken(dve, "cond", l, u)
                if key:
                    bank, free = filled(dve, *key)
                    tt(hs[:, t, cols], bank[:], mod[:, gate * D + 512 * half:gate * D + 512 * half + 512],
                       ALU.mult).then_inc(free, 1)
                    taken(dve, *key)
                else:
                    V.then(tt(hs[:, t, cols], ysum[:, t, cols],
                              mod[:, gate * D + 512 * half:gate * D + 512 * half + 512], ALU.mult))
                V.do(stt(hs[:, t, cols], xs[:, t, cols], ALPHA, hs[:, t, cols], ALU.mult, ALU.add))

            def layer_norm(stage):
                V.wait()
                for t in range(NT):
                    for k in range(2):
                        V.do(nc.vector.bn_stats(stats[:, t, k], hs[:, t, 512 * k:512 * k + 512]))
                for t in range(NT):
                    V.wait()
                    nc.vector.bn_aggr(aggr[:, t], stats[:, t]).then_inc(S["resid_var"], 1)
                dve.wait_ge(S["ln_in"], 32 * (stage + 1))
                for t in range(NT):
                    dve.wait_ge(S["resid_rstd"], NT * stage + t + 1)
                    V.then(nc.vector.reciprocal(rstd[:, t:t + 1], rstd[:, t:t + 1]))
                    V.then(ts(hs[:, t], hs[:, t], aggr[:, t, 0:1], rstd[:, t:t + 1], ALU.subtract, ALU.mult))
                    V.then(tt(hs[:, t], hs[:, t], ln[:, 0], ALU.mult))
                    tt(xs[:, t], hs[:, t], ln[:, 1], ALU.add).then_inc(S["ln_done"], 1)
                dve.wait_ge(S["ln_done"], NT * stage + NT)

            for u in range(4):
                cond(0, u)
            dve.wait_ge(S["x_in"], 16)
            modulate(0, 0)
            cond(0, 4)
            for t in range(NT):
                taken(dve, "ab", t)
            dve.wait_ge(S["gates_in"], 32)
            as8 = lambda a: a.rearrange("p (t h) -> p t h", t=NT)
            V.then(tt(as8(g_c), ab[:, :, 0:GH], over_all(dtb, NT), ALU.add))
            stt(g_a, g_c, -1.0, g_c, ALU.mult, ALU.max).then_inc(S["gate_in"], 1)
            ts(as8(g_b), ab[:, :, GH:2 * GH], -1.0, 80.0, ALU.mult, ALU.min).then_inc(S["gate_in"], 1)
            cond(0, 5)
            taken(dve, "convT")
            for i in range(3):
                for u in range(2):
                    taken(dve, "ev_in", i, u)
                for j in range(CONV_W):
                    for ch in range(GH * i, GH * i + GH):
                        w = conv_w[:, j * NF + ch:j * NF + ch + 1]
                        if j == 0:
                            last = ts(conv_y[:, ch], conv_x[:, ch, 0:SEQ], w, None, ALU.mult)
                        else:
                            last = stt(conv_y[:, ch], conv_x[:, ch, j:j + SEQ], w, conv_y[:, ch], ALU.mult, ALU.add)
                        if (j, ch) != (CONV_W - 1, GH * i + GH - 1):
                            V.do(last)
                    if j < CONV_W - 1:
                        V.wait()
                last.then_inc(S["conv_done"], 1)
            dve.wait_ge(S["gate_exp"], 3)
            V.then(ts(g_b, g_b, 1.0, None, ALU.add))
            V.do(nc.vector.reciprocal(beta, g_b))
            V.then(ts(g_d, g_a, 2.0, None, ALU.add))
            V.then(nc.vector.reciprocal(g_d, g_d))
            V.then(tt(g_a, g_a, g_d, ALU.mult))
            V.then(tt(g_b, g_a, g_a, ALU.mult))
            V.then(ts(g_d, g_b, 1.0 / 17, None, ALU.mult))
            for n in range(15, 1, -2):
                V.then(stt(g_d, g_d, 1.0 / n, g_b, ALU.add, ALU.mult))
            V.then(stt(g_d, g_d, 1.0, g_a, ALU.add, ALU.mult))
            V.then(ts(g_c, g_c, 0.0, None, ALU.max))
            V.then(stt(g_d, g_d, 2.0, g_c, ALU.mult, ALU.add))
            V.then(stt(as8(g_tok), as8(g_d), -1.0, over_all(alog, NT), ALU.mult, ALU.mult))
            tt(g_rhs, per_row(g_tok, P), over_all(cpart["upto"], NTH), ALU.mult).then_inc(S["g_rhs"], 1)
            tt(b_rhs, per_row(beta, P), over_all(ident, NTH), ALU.mult).then_inc(S["b_rhs"], 1)
            cond(0, 6)
            for i in range(4):
                taken(dve, "l2", i)
                n_i = norm[:, 512 * i:512 * i + 512]
                V.then(nc.vector.reciprocal(n_i, n_i))
                y_i = conv_y[:, 2 * i:2 * i + 2]
                stt(y_i, y_i, GD ** -0.5 if i < 2 else 1.0, n_i.rearrange("p (c t) -> p c t", c=2),
                    ALU.mult, ALU.mult).then_inc(S["qk_norm"], 1)
            dve.wait_ge(S["qk_norm"], 4)
            for t in range(NT):
                taken(dve, "ev_in", 4, t)
                taken(dve, "ev_in", 5, t)
            dve.wait_ge(S["trig_ready"], 2)
            col = lambda a: a[:, :, RK // 2:].unsqueeze(2).broadcast_to([P, NT, SH + SKV, SROT])
            x1, x2 = att_qk[:, :, :, 0:SROT], att_qk[:, :, :, SROT:2 * SROT]
            for to, a, b in ((0, x1, cos_t), (1, x2, sin_t), (2, x2, cos_t), (3, x1, sin_t)):
                V.do(tt(rope_tmp[to], a, col(b), ALU.mult))
            V.wait()
            tt(x1, rope_tmp[0], rope_tmp[1], ALU.subtract).then_inc(S["rope_done"], 1)
            tt(x2, rope_tmp[2], rope_tmp[3], ALU.add).then_inc(S["rope_done"], 1)
            for t in range(NT):
                bank, free = filled(dve, "g_row", t)
                dve.wait_ge(S["exp_row"], t + 1)
                V.then(tt(quad(dec, t), heads(bank), over_all(ident, GH), ALU.mult))
                V.then(nc.vector.tensor_reduce(quad(g_col, t), quad(dec, t), AX.X, ALU.add))
                for h in range(GH):
                    n = GH * t + h
                    last = stt(dec[:, n], bank[:, h * P:(h + 1) * P], g_col[:, n:n + 1], cpart["upto"],
                               ALU.subtract, ALU.mult)
                    if h < GH - 1:
                        V.do(last)
                last.then_inc(free, 1)
            for t in range(NT):
                bank, free = filled(dve, "b_row", t)
                tt(quad(kbT, t), by_tile(GH, t), heads(bank), ALU.mult).then_inc(free, 1)
            for t in range(NT):
                dve.wait_ge(S["dec_exp"], t + 1)
                V.do(tt(quad(dec, t), quad(dec, t), over_all(cpart["upto"], GH), ALU.mult))
            dve.wait_ge(S["e_col"], 1)
            V.then(tt(bg, beta, e_col, ALU.mult))
            taken(dve, "g_after")
            for t in range(NT):
                bank, free = filled(dve, "k_tok", t)
                V.do(tt(quad(kbg, t), heads(bank), per_row(quad(bg, t), P), ALU.mult))
                tt(quad(kdec, t), heads(bank), per_row(quad(e_after, t), P), ALU.mult).then_inc(free, 1)
            for t in range(NT):
                bank, free = filled(dve, "v_tok", t)
                tt(quad(vb, t), heads(bank), per_row(quad(beta, t), P), ALU.mult).then_inc(free, 1)
            for name, to in (("kk", aD), ("qk", qkT)):
                for t in range(NT):
                    if name == "kk":
                        filled(dve, "v_tok", NT - 1)
                    bank, free = filled(dve, name, t)
                    tt(quad(to, t), heads(bank), quad(dec, t), ALU.mult).then_inc(free, 1)
            for t in range(NT):
                dve.wait_ge(S["level_mask"], t + 1)
                tt(quad(Y, t), over_all(ident, GH), quad(amasks[0], t), ALU.subtract).then_inc(S["y0_ready"], 1)

            def block_scores(b):
                mask = cpart["att_prev" if b == 1 else "att_own"]
                for v in range(SKV):
                    bank, free = filled(dve, "score", b, v)
                    stt(scores[:, b, SG * v:SG * v + SG], heads(bank), SD ** -0.5, over_all(mask, SG),
                        ALU.mult, ALU.add).then_inc(free, 1)
                    taken(dve, "score", b, v)
                V.then(nc.vector.tensor_reduce(mx3[:, b], scores[:, b], AX.X, ALU.max))

            def subtract_max(b):
                tt(scores[:, b], scores[:, b], per_row(mx[:, BLOCKS[b][0]], P), ALU.subtract).then_inc(S["score_sub"], 1)

            def attention(l):
                if l == 1:
                    dve.wait_ge(S["sinks_in"], 16)
                    V.do(tt(mx[:, 0], mx3[:, 0], sinks, ALU.max))
                    V.then(tt(mx[:, 1], mx3[:, 1], mx3[:, 2], ALU.max))
                    V.then(tt(mx[:, 1], mx[:, 1], sinks, ALU.max))
                    tt(es, over_all(sinks, NT), mx, ALU.subtract).then_inc(S["sink_sub"], 1)
                    for b in range(3):
                        subtract_max(b)

            for b in range(3):
                block_scores(b)
            for l in range(1, N_LEVELS):
                if l < N_LEVELS - 1:
                    for t in range(NT):
                        bank, free = filled(dve, "xax", l, t)
                        taken(dve, *(("xax", l - 1, t) if l > 1 else ("xt", t)))
                        tt(quad(X, t), quad(X, t), heads(bank), ALU.subtract).then_inc(free, 1)
                for t in range(NT):
                    bank, free = filled(dve, "yay", l, t)
                    if l > 1:
                        taken(dve, "yay", l - 1, t)
                    else:
                        dve.wait_ge(S["y0_ready"], t + 1)
                    tt(quad(Y, t), quad(Y, t), heads(bank), ALU.subtract).then_inc(free, 1)
                attention(l)
                cond(0, 6 + l)
            taken(dve, "u", 0)
            nc.vector.tensor_copy(vn[0:CHUNK, 0:GH], U[0:CHUNK, 0:GH]).then_inc(S["v_first"], 1)
            for n in range(4):
                t, rows = n // 2, slice(CHUNK * (n % 2), CHUNK * (n % 2) + CHUNK)
                if n:
                    bank, free = filled(dve, "ws", n)
                    taken(dve, "u", t)
                    tt(quad(vn[rows], t), quad(U[rows], t), heads(bank)[rows], ALU.subtract).then_inc(free, 1)
                if n < 3:
                    bank, free = filled(dve, "kv", n)
                    if n == 0:
                        nc.vector.tensor_copy(state[:, 1], heads(bank)).then_inc(free, 1)
                    else:
                        taken(dve, "kv", n - 1)
                        for h in range(GH):
                            end = rows.stop - 1
                            last = stt(state[:, n + 1, h], state[:, n, h], eG[:, GH * t + h, end:end + 1],
                                       bank[:, h * P:(h + 1) * P], ALU.mult, ALU.add)
                            if h < GH - 1:
                                V.do(last)
                        last.then_inc(free, 1)
            for b in range(3):
                dve.wait_ge(S["prob_exp"], b + 1)
                V.do(nc.vector.tensor_reduce(sm3[:, b], scores[:, b], AX.X, ALU.add))
            dve.wait_ge(S["sink_exp"], 1)
            V.wait()
            V.do(tt(es[:, 0], es[:, 0], sm3[:, 0], ALU.add))
            V.then(tt(es[:, 1], es[:, 1], sm3[:, 1], ALU.add))
            V.then(tt(es[:, 1], es[:, 1], sm3[:, 2], ALU.add))
            V.then(nc.vector.reciprocal(es, es))
            for t in range(NT):
                bank, free = filled(dve, "pv", t)
                tt(om[:, t, GH * GD:].rearrange("p (h d) -> p h d", d=SD), bank[:].rearrange("p (h d) -> p h d", d=SD),
                   per_row(es[:, t], SD), ALU.mult).then_inc(free, 1)
            for t in range(NT):
                taken(dve, "go", t)
                V.then(tt(quad(o_sq, t), quad(o_tok, t), quad(o_tok, t), ALU.mult))
                nc.vector.tensor_reduce(quad(ssq, t), quad(o_sq, t), AX.X, ALU.add).then_inc(S["ssq_ready"], 1)
            for t in range(NT):
                taken(dve, "pv", t)
                dve.wait_ge(S["o_rstd"], t + 1)
                V.then(nc.vector.reciprocal(quad(rstd_o, t), quad(rstd_o, t)))
                V.then(tt(quad(o_tok, t), quad(o_tok, t), per_row(quad(rstd_o, t), P), ALU.mult))
                dve.wait_ge(S["z_w"], t + 1)
                tt(om[:, t, 0:GH * GD].rearrange("p (h d) -> p h d", h=GH), quad(o_tok, t),
                   zs[:, t].rearrange("p (h d) -> p h d", h=GH), ALU.mult).then_inc(S["mix_ready"], 1)
            for u in range(2):
                for t in range(NT):
                    residual(0, 2, ("ev_out", u, t), t, u)
            layer_norm(0)
            modulate(0, 3)
            for u in range(FFN // 256):
                for t in range(NT):
                    bank, free = filled(dve, "ffn_up", u, t)
                    dve.wait_ge(S["ffn_silu"], NT * u + t + 1)
                    if u >= 2:
                        filled(dve, "ffn_T", u - 2)
                    tt(ff_a[:, u % 2, t], ff_s[:, u % 2, t], bank[:, 256:512], ALU.mult).then_inc(free, 1)
                if u < 10:
                    cond(1, u)
            for t in range(NT):
                for half in range(2):
                    residual(0, 5, ("ffn_down", t, half), t, half)
            layer_norm(1)
            modulate(1, 0)
            cond(1, 10)
            cond(1, 11)
            for h in range(RH + 1):
                if h < RH:
                    for t in range(NT):
                        bank, free = filled(dve, "od_qk", h, t)
                        x1, x2 = (bank[:].rearrange("p (a n) -> p a n", a=2)[:, :, i * P:(i + 1) * P] for i in range(2))
                        tabs = [over_all(a[:, t, 0:P], 2) for a in (cos_t, sin_t)]
                        if NT * h + t:
                            dve.wait_ge(S["od_rope"], NT * h + t)
                        V.do(tt(r_tmp[0], x1, tabs[0], ALU.mult))
                        V.do(tt(r_tmp[1], x2, tabs[1], ALU.mult))
                        V.do(tt(r_tmp[2], x2, tabs[0], ALU.mult))
                        tt(r_tmp[3], x1, tabs[1], ALU.mult).then_inc(free, 1)
                        taken(dve, "od_qk", h, t)
                        if h:
                            filled(dve, "ret_T", h - 1, t)
                        V.do(tt(r_qk[:, t, :, 0:P], r_tmp[0], r_tmp[1], ALU.subtract))
                        tt(r_qk[:, t, :, P:2 * P], r_tmp[2], r_tmp[3], ALU.add).then_inc(S["od_rope"], 1)
                if h:
                    g = h - 1
                    for t in range(NT):
                        bank, _ = filled(dve, "ret_y", g, t)
                        V.then(nc.vector.bn_stats(stats[:, t, 0], bank[:]))
                        nc.vector.bn_aggr(aggr[:, t], stats[:, t, 0]).then_inc(S["ret_var"], 1)
                    for t in range(NT):
                        dve.wait_ge(S["ret_rstd"], NT * g + t + 1)
                        V.then(nc.vector.reciprocal(rstd[:, t:t + 1], rstd[:, t:t + 1]))
                        if g:
                            filled(dve, "ret_yT", g - 1, t)
                        bank, free = filled(dve, "ret_y", g, t)
                        ts(r_y[:, t], bank[:], aggr[:, t, 0:1], rstd[:, t:t + 1], ALU.subtract, ALU.mult).then_inc(free, 1)
                        taken(dve, "ret_y", g, t)
                        dve.wait_ge(S["od_gate"], NT * g + t + 1)
                        tt(r_y[:, t], r_y[:, t], r_g[:, g % 2, t], ALU.mult).then_inc(S["ret_y"], 1)
                if h < RH:
                    dve.wait_ge(S["ret_in"], 16)
                    bank, free = filled(dve, "ret_s", h)
                    V.do(tt(r_s[:, 0:2 * P], bank[:, 0:2 * P], ret_d[:, h], ALU.mult))
                    tt(r_s[:, 2 * P:3 * P], bank[:, 2 * P:3 * P], ret_d[:, h, 0:P], ALU.mult).then_inc(free, 1)
            for t in range(NT):
                for half in range(2):
                    residual(1, 2, ("od_out", t, half), t, half)
            layer_norm(2)
            modulate(1, 3)
            dve.wait_ge(S["late_in"], 16)
            bank, free = filled(dve, "router")
            tt(logit, bank[:, 0:NT * NE].rearrange("p (t e) -> p t e", t=NT), over_all(rb, NT), ALU.add).then_inc(free, 1)
            taken(dve, "router")
            iota8 = over_all(iota[:, 0:NE], NT)
            for lg, m, first, eq in ((logit, m1, i1, eq1), (l2, m2, i2, eq2)):
                V.then(nc.vector.tensor_reduce(m, lg, AX.X, ALU.max))
                V.then(tt(key_, lg, per_row(m, NE), ALU.is_equal))
                V.then(stt(key_, key_, -100.0, iota8, ALU.mult, ALU.add))
                V.then(nc.vector.tensor_reduce(first, key_, AX.X, ALU.min))
                V.then(tt(eq, key_, per_row(first, NE), ALU.is_equal))
                if lg is logit:
                    V.then(stt(l2, eq, NEG, logit, ALU.mult, ALU.add))
            tt(e12, m2, m1, ALU.subtract).then_inc(S["route_in"], 1)
            mask2 = table[:, 2:4, 0:NE]
            tt(mask2, eq1, eq2, ALU.add).then_inc(S["rank_in"], 1)
            dve.wait_ge(S["route_exp"], 1)
            V.then(ts(w1, e12, 1.0, None, ALU.add))
            V.then(nc.vector.reciprocal(w1, w1))
            V.then(tt(w2, e12, w1, ALU.mult))
            V.then(tt(eq1, eq1, per_row(w1, NE), ALU.mult))
            V.then(tt(eq2, eq2, per_row(w2, NE), ALU.mult))
            for i in range(2):
                V.do(tt(table[:, 4:6, NE * i:NE * i + NE], eq1, eq2, ALU.add))
            dve.wait_ge(S["rank_in"], 1)
            V.do(nc.vector.tensor_copy(table[:, 2:4, NE:], mask2))
            bank, free = filled(dve, "rank")
            places = bank[:, 0:NT * NE].rearrange("p (t e) -> p t e", t=NT)
            V.do(nc.vector.tensor_copy(table[:, 0:2, 0:NE], places))
            V.do(ts(table[:, 0:2, NE:], places, -float(P), None, ALU.add))
            nc.vector.tensor_copy(cnt, bank[:, NT * NE:NT * NE + NE]).then_inc(free, 1)
            taken(dve, "rank")
            V.then(ts(over, cnt, float(P), None, ALU.is_gt))
            src, dst = over, rank_o
            for d in (1, 2, 4):
                V.do(nc.vector.tensor_copy(dst[:, 0:d], src[:, 0:d]))
                V.then(tt(dst[:, d:], src[:, d:], src[:, 0:NE - d], ALU.add))
                src, dst = dst, (cnt if dst is rank_o else rank_o)
            V.do(nc.vector.tensor_copy(code[:, 0:NE], iota[:, 0:NE]))
            V.then(stt(code[:, NE:], src, float(NE), over, ALU.add, ALU.mult))
            V.then(ts(code[:, NE:], code[:, NE:], -1.0, None, ALU.add))
            for i in range(MAX_OVER):
                V.then(ts(over_hot[:, i], code[:, NE:], float(NE + i), None, ALU.is_equal))
                V.do(tt(over_hot[:, i], over_hot[:, i], iota[:, 0:NE], ALU.mult))
            V.wait()
            V.do(nc.vector.tensor_copy(over_int[0:1, 3:4], src[0:1, NE - 1:NE]))
            V.then(nc.vector.tensor_reduce(over_id, over_hot, AX.X, ALU.add))
            nc.vector.tensor_copy(over_int[0:1, 0:3], over_id[0:1, :]).then_inc(S["over_ready"], 1)
            V.do(nc.vector.memset(item_no, 0.0))
            for t in range(NT):
                V.do(nc.vector.memset(ysum[:, t], 0.0))
            nc.vector.memset(pwT, 0.0).then_inc(S["back_zero"], 1)
            nc.vector.memset(ye[:], 0.0).then_inc(S["back_zero"], 1)
            V.wait()

            def build():
                V.then(ts(hot, code, item_no, None, ALU.is_equal))
                V.do(ts(item_no, item_no, 1.0, None, ALU.add))
                V.then(tt(pick, table, over_all(hot, 6), ALU.mult))
                V.then(nc.vector.tensor_reduce(picked, pick, AX.X, ALU.add))
                for t in range(NT):
                    V.do(ts(p_tok[:, t], iota, picked[:, t:t + 1], picked[:, 2 + t:3 + t], ALU.is_equal, ALU.mult))
                for t in range(NT):
                    last = ts(pw_tok[:, t], iota, picked[:, t:t + 1], picked[:, 4 + t:5 + t], ALU.is_equal, ALU.mult)
                    if t < NT - 1:
                        V.do(last)
                last.then_inc(S["p_ready"], 1)

            BUILD_STEPS = 7
            n0 = V.n
            build()
            assert V.n - n0 == BUILD_STEPS
            steps_before = V.n

            def rest(it, n, slot, buf):
                split(dve, "w_hi", it, n + 1)
                at = ring[:, slot * UNIT + (n % 2) * PIECE:slot * UNIT + (n % 2 + 1) * PIECE]
                tt(w_lo[:, buf], at, w_hi[:, buf].bitcast(F32), ALU.subtract).then_inc(S["w_lo"], 1)

            def add_back(it):
                for i in range(4):
                    item_taken(dve, it, "back", i, ago=1)
                    bank, free = item_filled(dve, it, "back", i)
                    to = ysum[:, i // 2, 512 * (i % 2):512 * (i % 2) + 512]
                    tt(to, to, bank[:], ALU.add).then_inc(free, 1)

            def item(it, late=0):
                def split_unit(u):
                    for n in (2 * (u + late), 2 * (u + late) + 1):
                        rest(it, n, n // 2 % RING, n % 3)

                if late:
                    split_unit(0)
                for u in range(N_UNITS):
                    if 1 <= u <= N_UP:
                        bank, free = item_filled(dve, it, "up", u - 1)
                        dve.wait_ge(S["e_silu"], it * N_UP + u)
                        item_filled(dve, it, "act_T", (u - 3) % N_UP, ago=int(u < 3))
                        tt(e_a[:, (u - 1) % 2], e_s[:, (u - 1) % 2], bank[:, 256:512], ALU.mult).then_inc(free, 1)
                    if u < N_UNITS - late:
                        split_unit(u + 1)
                    if u == 0:
                        add_back(it)
                        item_filled(dve, it, "pwT")
                        V.n, V.base = 0, it * BUILD_STEPS + steps_before
                        build()
                    if 1 <= u <= N_UP:
                        dve.wait_ge(S["act_hi"], it * N_UP + u)
                        bank, free = item_filled(dve, it, "act_T", u - 1)
                        to = slice(2 * u - 2, 2 * u)
                        tt(eT_lo[:, to], bank[:, 0:256].rearrange("p (j s) -> p j s", j=2),
                           eT_hi[:, to].bitcast(F32), ALU.subtract).then_inc(free, 1)
                    if u == N_UP + 1:
                        for half in range(2):
                            tokens_lo(half, item_filled(dve, it, "gather", half), it * 2 + (3 + half))

            def tokens_lo(half, bank_free_, count):
                bank, free = bank_free_
                dve.wait_ge(S["tok_hi"], count)
                to = slice(4 * half, 4 * half + 4)
                tt(heT_lo[:, to], heads(bank), heT_hi[:, to].bitcast(F32), ALU.subtract).then_inc(free, 1)

            for half in range(2):
                tokens_lo(half, filled(dve, "gather", half), 1 + half)
            for n in range(2):
                rest(0, n, 0, n)
            with dve.Fori(0, NE) as it:
                item(it)
            over_loop(dve, lambda it: item(it, 1))
            add_back(dve.value_load(over_int[0:1, 3:4], min_val=0, max_val=MAX_OVER) + NE)
            V = Steps(dve, S["last_step"])
            V.then(nc.vector.memset(item_no, 0.0))
            for t in range(NT):
                for half in range(2):
                    residual(1, 5, None, t, half)
            layer_norm(3)

        @block.gpsimd
        def _(pool):
            tt = nc.gpsimd.tensor_tensor
            quad = lambda a, t: a[:, GH * t:GH * t + GH]
            pool.dma_start(alog, ev_a_log.broadcast_to([P, GH])).then_inc(S["gates_in"], 16)
            pool.dma_start(dtb, ev_dt_bias.broadcast_to([P, GH])).then_inc(S["gates_in"], 16)
            pool.dma_start(sinks, ev_sinks.broadcast_to([P, SH])).then_inc(S["sinks_in"], 16)
            pool.dma_start(gdnw, ev_gdn_norm_w.broadcast_to([P, GD])).then_inc(S["gdnw_in"], 16)

            def load_ln(stage):
                for i, w in enumerate((ln_w, ln_b)):
                    pool.dma_start(ln[:, i], w[stage // 2, stage % 2:stage % 2 + 1, :].broadcast_to([P, D])) \
                        .then_inc(S["ln_in"], 16)

            pool.wait_ge(S["qk_norm"], 2)
            for t in range(NT):
                pool.wait_ge(S["exp_row"], t + 1)
                tt(quad(qdT, t), by_tile(0, t), quad(eG, t), ALU.mult).then_inc(S["q_dec"], 1)
            pool.wait_ge(S["gdnw_in"], 16)

            def level(l):
                for t in range(NT):
                    if l == 0:
                        pool.wait_ge(S["trig_ready"], 2)
                        taken(pool, "kk", t)
                    elif l == 2:
                        pool.wait_ge(S["y0_ready"], t + 1)
                    elif l > 2:
                        filled(pool, "ax", l - 2, t)
                    tt(quad(amasks[l % 2], t), quad(aD, t), over_all(cpart["levels"][:, l * P:(l + 1) * P], GH),
                       ALU.mult).then_inc(S["level_mask"], 1)

            for l in range(4):
                level(l)
            for t in range(NT):
                taken(pool, "ev_in", 3, t)
                z = zs[:, t].rearrange("p (h d) -> p h d", h=GH)
                tt(z, z, over_all(gdnw, GH), ALU.mult).then_inc(S["z_w"], 1)
            level(4)
            level(5)
            filled(pool, "pv", NT - 1)
            load_ln(0)
            pool.wait_ge(S["ln_done"], NT)
            load_ln(1)
            filled(pool, "ffn_down", NT - 1, 1)
            pool.dma_start(ret_d, consts[:, CONST_COLS - RH * 2 * P:].rearrange("p (h n) -> p h n", h=RH)).then_inc(S["ret_in"], 16)
            pool.dma_start(gnw.rearrange("p h n -> p (h n)"), od_gn_w.broadcast_to([P, RH * RV])).then_inc(S["gnw_in"], 16)
            pool.wait_ge(S["ln_done"], 2 * NT)
            load_ln(2)
            pool.wait_ge(S["gnw_in"], 16)
            for h in range(RH):
                for t in range(NT):
                    taken(pool, "od_g", h, t)
                    tt(r_g[:, h % 2, t], r_g[:, h % 2, t], gnw[:, h], ALU.mult).then_inc(S["od_gate"], 1)
                if h == 0:
                    pool.wait_ge(S["h_ready"], 6)
                    pool.dma_start(late, consts[:, N_RING:N_RING + 2 * P]).then_inc(S["late_in"], 16)
                    pool.dma_start(rw, moe_w_router[0].rearrange("(k p) e -> p k e", p=P)).then_inc(S["router_in"], 16)
                    pool.dma_start(rb, moe_b_router.broadcast_to([P, NE])).then_inc(S["router_in"], 16)
            pool.wait_ge(S["ln_done"], 3 * NT)
            load_ln(3)


_INS = ["x", "c", "positions", "cond_w", "cond_b", "ln_w", "ln_b", "ev_w_in", "ev_conv_w", "ev_a_log", "ev_dt_bias",
        "ev_gdn_norm_w", "ev_sinks", "ev_w_out", "ffn_w_up", "ffn_w_down", "od_w_in", "od_gn_w", "od_w_out",
        "moe_w_router", "moe_b_router", "moe_w_up", "moe_w_down"]


def kernel(**inputs):
    import concourse.bacc as bacc
    from concourse.bass_utils import run_bass_kernel_spmd

    nc = bacc.Bacc("TRN2", target_bir_lowering=False, num_devices=1)
    arrays = {f"in_{n}": np.ascontiguousarray(inputs[n]) for n in _INS}
    arrays["in_consts"] = np.concatenate(
        [np.asarray(v, np.float32) for v in constant_table().values()], axis=1)
    args = [nc.dram_tensor(n, a.shape, mybir.dt.from_np(a.dtype), kind="ExternalInput").ap() for n, a in arrays.items()]
    out = nc.dram_tensor("out_y", (1, SEQ, D), F32, kind="ExternalOutput").ap()
    trunk(nc, *args, out)
    r = run_bass_kernel_spmd(nc, [arrays], core_ids=[0])
    return r.results[0]["out_y"]
```

```python
from contextlib import ExitStack

import numpy as np

import concourse.bass as bass
from concourse import mybir

ALU = mybir.AluOpType
ACT = mybir.ActivationFunctionType
AX = mybir.AxisListType
F32 = mybir.dt.float32
F32R = mybir.dt.float32r
I32 = mybir.dt.int32

P = 128
D = 1024
SEQ = 256
NT = SEQ // P
KC = D // P
CHUNK = 64
GH, GD = 4, 128
NTH = NT * GH
CONV_W = 4
QKV = 3 * GH * GD
NF = QKV // P
SH, SKV, SD = 8, 2, 64
SG = SH // SKV
SROT = SD // 8
RH, RK, RV = 4, 256, 512
FFN = 2816
NE = 8
FFE = 3584
UNIT = 4096
RING = 3
PIECE = UNIT // 2
PART = UNIT // 4
BUFS = 3
ARENA = 25344
ALPHA = 4.0 ** 0.25
LN_EPS = 1e-5
NORM_EPS = 1e-6
NEG = -1e30
N_LEVELS = 6
TWO_PI = 2.0 * np.pi
PI2_A = 6.28125
PI2_B = float(np.float32(np.round((TWO_PI - PI2_A) * 2.0 ** 20) / 2.0 ** 20))
PI2_C = float(np.float32(TWO_PI - PI2_A - PI2_B))
ROUND = 1.5 * 2.0 ** 23
PI_MAX = 3.1415925

NFREQ = RK // 2 + SROT
LATE = ("strict", "iota", "ret")


def constant_table():
    s, t = np.arange(P)[:, None], np.arange(P)[None, :]
    same = (s // CHUNK) == (t // CHUNK)
    parts = {
        "ident": s == t,
        "ones": np.ones((P, P)),
        "upto": (s <= t) & same,
        "after": (s > t) & same,
        "att_own": np.where((s < CHUNK) & (t >= CHUNK), NEG, 0.0),
        "att_prev": np.where((s < CHUNK) & (t >= CHUNK), 0.0, NEG),
        "levels": np.concatenate(
            [((t // b) % 2 == 1) & ((s // b) == (t // b) - 1) for b in (1 << n for n in range(N_LEVELS))], 1
        ),
    }
    half_r, half_s = RK // 2, SROT
    f = np.concatenate([
        np.float32(10000.0) ** (-np.arange(half_r, dtype=np.float32) / np.float32(half_r)),
        np.float32(500000.0) ** (-np.arange(half_s, dtype=np.float32) / np.float32(half_s)),
    ])
    parts["freq"] = np.broadcast_to(f[None, :], (P, NFREQ))
    parts["strict"] = s < t
    parts["iota"] = np.broadcast_to(t, (P, P))
    ret = np.zeros((P, RH, 2, P))
    for h in range(RH):
        log_g = np.log1p(-(2.0 ** (-5.0 - h)))
        dist = (t - s).astype(np.float64)
        ret[:, h, 0] = np.where(dist >= 0, np.exp(np.maximum(dist, 0) * log_g), 0.0)
        ret[:, h, 1] = np.exp((dist + P) * log_g)
    parts["ret"] = ret.reshape(P, -1) * RK ** -0.5
    return parts


def psum_plan(plan):
    at, count, turn = {}, [0] * 8, 0

    def use(*key):
        nonlocal turn
        at[key] = (turn % 8, count[turn % 8])
        count[turn % 8] += 1
        turn += 1

    for key in plan:
        use(*key)
    return at, count


FIRST_COND = (2, 0, 3, 1)
UP_COND = {0: (0, 10), 2: (0, 11), 3: (1, 0), 5: (1, 1), 6: (1, 2), 8: (1, 3), 9: (1, 4)}
DOWN_COND = {0: (1, 5), 2: (1, 6), 3: (1, 7)}
OD_COND = {0: 8, 1: 9, 2: 10, 3: 11}


def stream_units():
    c = lambda l, *n: [("cond", l, i) for i in n]
    e = lambda *n: [("ev_in", i) for i in n]
    order = c(0, *FIRST_COND) + e(0, 1, 2, 5, 4, 3) + c(0, 4, 5, 6, 7, 8, 9)
    order += [("ev_out", 0), ("ev_out", 1)]
    for i in range(FFN // 256):
        order += [("ffn_up", i)] + ([("cond", *UP_COND[i - 1])] if i - 1 in UP_COND else [])
    for i in range(6):
        order += [("ffn_down", i)] + ([("cond", *DOWN_COND[i - 1])] if i - 1 in DOWN_COND else [])
    for h in range(RH):
        order += [("od_qk", h), ("od_v", h), ("od_g", h)] + c(1, OD_COND[h])
    order += [("od_out", i) for i in range(4)]
    return order


def by_pool(unit, j):
    if unit[0] == "ev_in":
        return j % 2 == 1 or unit[1] == 0
    return j == 3 or unit in (("ev_out", 0), ("ffn_up", 0), ("od_qk", 0))


def unit_parts(key):
    return 2 if key == ("ffn_down", 5) else 4


def pe_order():
    o = [("cT",)]
    o += [("cond", 0, u) for u in FIRST_COND] + [("convT",)] + [("hT", 0, i) for i in range(4)] + [("ab", t) for t in range(NT)]
    o += [("ev_in", u, i) for u in range(3) for i in range(4)]
    o += [("ev_in", u, t) for u in (5, 4, 3) for t in range(NT)]
    o += [("l2", i) for i in range(4)]
    o += [("g_row", t) for t in range(NT)] + [("b_row", t) for t in range(NT)] + [("g_after",)]
    o += [("k_tok", t) for t in range(NT)] + [("v_tok", t) for t in range(NT)]
    o += [("kk", t) for t in range(NT)] + [("qk", t) for t in range(NT)]
    o += [("xt", t) for t in range(NT)]
    o += [("att_T", i) for i in range(3)]
    for l in range(1, N_LEVELS):
        o += [("ax", l, t) for t in range(NT)]
        o += [("cond", 0, 2 + l)] if l > 1 else [("score", b, v) for b in range(3) for v in range(SKV)]
        o += [("xax", l, t) for t in range(NT)] if l < N_LEVELS - 1 else []
        o += [("yay", l, t) for t in range(NT)]
    o += [("u", t) for t in range(NT)] + [("w", t) for t in range(NT)] + [("cond", 0, 8)]
    o += [("prob_T", b, v) for b in range(3) for v in range(SKV)] + [("pv", t) for t in range(NT)] + [("cond", 0, 9)]
    for n in range(4):
        o += ([("ws", n)] if n else []) + ([("kv", n)] if n < 3 else [])
    o += [("go", t) for t in range(NT)]
    o += [("hT", 1, i) for i in (2, 3, 0, 1)]
    o += [("ev_out", u, t) for u in range(2) for t in range(NT)]
    o += [("hT", 2, i) for i in range(4)]
    for u in range(FFN // 256):
        o += [("ffn_up", u, t) for t in range(NT)] + ([("cond", *UP_COND[u - 1])] if u - 1 in UP_COND else [])
        o += [("ffn_T", u - 1)] if u else []
    o += [("ffn_down", t, h) for t in range(NT) for h in range(2)] + [("ffn_T", FFN // 256 - 1)]
    o += [("cond", *key) for key in DOWN_COND.values()]
    o += [("hT", 3, i) for i in range(4)]
    for h in range(RH):
        o += [("od_qk", h, t) for t in range(NT)]
        if h:
            o += [("cond", 1, OD_COND[h - 1])] + [("ret_y", h - 1, t) for t in range(NT)]
        o += [("od_v", h, t) for t in range(NT)] + [("ret_T", h, t) for t in range(NT)]
        o += [("od_g", h, t) for t in range(NT)] + [("ret_s", h)]
        if h:
            o += [("ret_yT", h - 1, t) for t in range(NT)]
    o += [("cond", 1, OD_COND[RH - 1])] + [("od_out", t, i) for t in range(NT) for i in range(2)]
    o += [("ret_y", RH - 1, t) for t in range(NT)] + [("ret_yT", RH - 1, t) for t in range(NT)]
    o += [("hT", 4, i) for i in range(4)]
    o += [("router",), ("rank",)]
    o += [("gather", 0), ("gather", 1)]
    return o


N_UP = FFE // 256
N_DOWN = FFE // P // 4
N_UNITS = N_UP + N_DOWN
MAX_OVER = 2 * SEQ // (P + 1)
N_ITEMS = NE + MAX_OVER


def item_plan():
    at, count = {}, [0] * 8

    def use(bank, *key):
        at[key] = (bank, count[bank])
        count[bank] += 1

    for u in range(N_UP):
        use(u % 3, "up", u)
        if u:
            use(3 + (u - 1) % 2, "act_T", u - 1)
        else:
            for i in range(4):
                use((6, 3, 4, 5)[i], "back", i)
            use(7, "pwT")
    use(3 + (N_UP - 1) % 2, "act_T", N_UP - 1)
    use(7, "down", 0)
    use(5, "down", 1)
    use(6, "gather", 0)
    use(2, "gather", 1)
    return at, count


class Steps:

    def __init__(self, eng, sem):
        self.eng, self.sem, self.n, self.base = eng, sem, 0, None

    def do(self, ins):
        ins.then_inc(self.sem, 1)
        self.n += 1
        return self.n

    def wait(self, n=None):
        n = self.n if n is None else n
        self.eng.wait_ge(self.sem, n if self.base is None else self.base + n)

    def then(self, ins):
        self.do(ins)
        self.wait()


SEMS = (
    "consts_in ident_in positions_in x_in c_in convw_in abw_in gates_in sinks_in bias_in gdnw_in ln_in gnw_in ret_in router_in late_in "
    "c_act pads_zero angle_ready trig_ready cond_acc h_ready gate_in gate_exp conv_done q_act k_act v_act squared "
    "qk_norm rope_done k_raw g_rhs b_rhs exp_row dec_exp e_col q_dec level_mask y0_ready score_sub sink_sub "
    "prob_exp sink_exp v_first ssq_ready o_rstd z_w mix_ready resid_var resid_rstd ln_done ffn_silu down_units "
    "od_rope od_gate ret_var ret_rstd ret_y route_in route_exp rank_in over_ready p_ready e_silu w_hi w_lo w_lo_pool "
    "turn_hi rows_hi nw_hi nw_lo zeroed piece_used act_hi tok_hi back_zero out_done "
    "dve_step last_step"
).split()


def trunk(nc, x, c, positions, cond_w, cond_b, ln_w, ln_b, ev_w_in, ev_conv_w, ev_a_log, ev_dt_bias,
          ev_gdn_norm_w, ev_sinks, ev_w_out, ffn_w_up, ffn_w_down, od_w_in, od_gn_w, od_w_out,
          moe_w_router, moe_b_router, moe_w_up, moe_w_down, consts, out):
    fills, fills_before = psum_plan(pe_order())
    item_at, item_uses = item_plan()
    widths = {k: v.shape[1] for k, v in constant_table().items()}
    early = [k for k in widths if k not in LATE]
    N_FIRST = sum(widths[k] for k in early)
    CONST_COLS = sum(widths.values())

    with ExitStack() as ctx:
        def sb(name, shape, dt=F32):
            return ctx.enter_context(nc.sbuf_tensor(name, shape, dt))

        S = {n: ctx.enter_context(nc.semaphore(n)) for n in SEMS}
        weights_in = [ctx.enter_context(nc.semaphore(f"weights_in{i}")) for i in range(RING)]
        bank_full = [ctx.enter_context(nc.semaphore(f"bank_full{i}")) for i in range(8)]
        bank_free = [ctx.enter_context(nc.semaphore(f"bank_free{i}")) for i in range(8)]
        banks = [ctx.enter_context(nc.psum_tensor(f"bank{i}", [P, 512], F32)) for i in range(8)]

        ring = sb("ring", [P, RING * UNIT])
        xs = sb("xs", [P, NT, D])
        hs = sb("hs", [P, NT, D])
        mod = sb("mod", [P, 6 * D])
        acc = sb("acc", [P, 2, 512])
        ln = sb("ln", [P, 2, D])
        cst = sb("cst", [P, N_FIRST])
        cpart, off = {}, 0
        for k in early:
            cpart[k] = cst[:, off:off + widths[k]]
            off += widths[k]
        ident, ones = cpart["ident"], cpart["ones"]
        small = sb("small", [P, 572])
        posi = sb("posi", [P, NT], I32)
        over_int = sb("over_int", [1, 4], I32)

        def overlay(at, *specs):
            made = []
            with ExitStack() as place:
                if at:
                    place.enter_context(nc.sbuf_tensor(f"before_{specs[0][0]}", [P, at], F32))
                for name, shape, dt in specs:
                    made.append(place.enter_context(nc.sbuf_tensor(name, shape, dt)))
            return made

        W_AT, LO_AT, OWN_AT, TRIG_AT = 2 * D, 2 * D + 2 * BUFS * PART, 4 * D + 2 * BUFS * PART, ARENA - 2 * NT * NFREQ
        hT_hi, w_part, hT_lo = overlay(0, ("hT_hi", [P, KC, SEQ], F32R), ("w_part", [P, BUFS, 2, PART], F32R),
                                       ("hT_lo", [P, KC, SEQ], F32R))
        ffT_hi, ffT_lo = overlay(OWN_AT, ("ffT_hi", [P, FFN // P, SEQ], F32R), ("ffT_lo", [P, FFN // P, SEQ], F32R))
        yT_hi, yT_lo = overlay(OWN_AT, ("yT_hi", [P, RH * RV // P, SEQ], F32R), ("yT_lo", [P, RH * RV // P, SEQ], F32R))
        w_hi, eT_hi, w_lo, eT_lo, heT_hi, heT_lo = overlay(
            W_AT, *((n + i, [P, *dims], F32R) for i in ("_hi", "_lo") for n, dims in (("w", (3, PIECE)), ("eT", (FFE // P, P)))),
            *((n, [P, KC, P], F32R) for n in ("heT_hi", "heT_lo")))
        nw_hi, nw_lo = overlay(TRIG_AT - 2 * KC * NE, *((n, [P, KC, NE], F32R) for n in ("nw_hi", "nw_lo")))
        MOE_AT = W_AT + 6 * PIECE + 2 * FFE + 2 * D
        arena = sb("arena", [P, ARENA])
        def carver(region):
            at = [0]

            def take(*dims):
                n = int(np.prod(dims))
                a = region[:, at[0]:at[0] + n]
                at[0] += n
                assert at[0] <= region.shape[1], (at[0], region.shape)
                if len(dims) == 1:
                    return a
                names = "abcde"[:len(dims)]
                return a.rearrange(f"p ({' '.join(names)}) -> p {' '.join(names)}",
                                   **{n_: d for n_, d in zip(names, dims)})
            return take

        def over_all(a, n):
            return a.unsqueeze(1).broadcast_to([P, n, a.shape[-1]])

        def per_row(a, n):
            return a.unsqueeze(2).broadcast_to([P, a.shape[-1], n])

        low, tiny = carver(arena[:, OWN_AT:TRIG_AT]), carver(small)
        up = low
        conv_flat = low(NF * 259)
        conv_x = conv_flat.rearrange("p (c t) -> p c t", c=NF)
        conv_y = low(NF, SEQ)
        norm = arena[:, LO_AT:LO_AT + 2048]
        part = carver(arena[:, W_AT:LO_AT])
        U, AXs, eG, dec, kbT, kbg = (part(NTH, P) for _ in range(6))
        kdec = low(NTH, P)
        trig = carver(arena[:, TRIG_AT:])(2, NT, NFREQ)
        vb, qdT = up(NTH, P), up(NTH, P)
        amask = up(2048)
        att_qk = up(NT, SH + SKV, SD)
        att_flat = att_qk.rearrange("p t h d -> p (t h d)")
        att_v, att_qT, att_kT = up(NT, SKV * SD), up(NT, SG, P), up(NT, P)
        th = lambda a: a.rearrange("p (n j) -> p n j", n=NTH)
        X, Y = th(norm[:, 0:1024]), th(norm[:, 1024:2048])
        amasks = [th(amask[:, 0:1024]), th(amask[:, 1024:2048])]
        g_rhs, b_rhs, wT, vn = amasks[0], amasks[1], kbT, amasks[0]
        conv_blocks = conv_y.rearrange("p c (t j) -> p (c t) j", t=NT)
        o_tok, o_sq, aD = conv_blocks[:, 0:8], conv_blocks[:, 8:16], conv_blocks[:, 16:24]
        kT = lambda t, h: conv_blocks[:, 2 * (GH + h) + t]
        qT = lambda t, h: conv_blocks[:, 2 * h + t]
        vT = lambda t, h: conv_blocks[:, 2 * (2 * GH + h) + t]
        om = hs
        by_tile = lambda lo, t: conv_y[:, lo:lo + GH, t * P:(t + 1) * P]
        zs = mod[:, 0:1024].rearrange("p (t n) -> p t n", t=NT)
        qkT = th(mod[:, 1024:2048])
        state = arena[:, 0:W_AT].rearrange("p (n h j) -> p n h j", n=4, h=GH)
        scores = conv_flat[:, 0:3072].rearrange("p (b h k) -> p b h k", b=3, h=SH)
        ln_flat = ln[:, :, :].rearrange("p a n -> p (a n)")
        pT = [r.rearrange("p (h q) -> p h q", h=SH)
              for r in (ln_flat[:, 0:1024], ln_flat[:, 1024:2048], att_flat[:, 0:1024])]
        ang_take = carver(amask)
        ang = [ang_take(NT, NFREQ) for _ in range(4)]
        sin_t, cos_t = trig[:, 0], trig[:, 1]
        rope_take = carver(norm)
        rope_tmp = [rope_take(NT, SH + SKV, SROT) for _ in range(4)]
        conv_rows = vb[0:CONV_W * NF, 0]
        c_row = vb[0:KC, 1]
        conv_w = tiny(48)
        ab_w = tiny(KC, 8)
        gdnw = tiny(P)
        bias_rows = tiny(P)
        cT, eps_n, eps_ln = tiny(KC), tiny(1), tiny(1)
        posf = tiny(NT)
        beta, g_tok, g_col, e_after, bg, e_col, ssq, rstd_o = (tiny(NTH) for _ in range(8))
        ab = tiny(NT, 8)
        g_a, g_b, g_c, g_d = (tiny(NTH) for _ in range(4))
        alog, dtb = tiny(GH), tiny(GH)
        stats, aggr, rstd = tiny(NT, 2, 6), tiny(NT, 2), tiny(NT)
        sinks, mx3, sm3, mx, es = low(SH), low(3, SH), low(3, SH), low(NT, SH), low(NT, SH)

        low = carver(arena[:, OWN_AT + 2 * FFN // P * SEQ:TRIG_AT])
        ff_s, ff_a = low(2, NT, 256), low(2, NT, 256)

        low = carver(arena[:, OWN_AT + 2 * RH * RV // P * SEQ:TRIG_AT])
        ret_d, gnw, r_qk, r_qT = low(RH, 2 * P), low(2, RV), low(NT, 2, RK), low(4, SEQ)
        r_s, r_y = low(3 * P), low(NT, RV)
        r_v = hs[:, :, :].rearrange("p t n -> p (t n)").rearrange("p (a t n) -> p a t n", a=2, t=NT)
        r_g = ln[:, :, :].rearrange("p t n -> p (t n)").rearrange("p (a t n) -> p a t n", a=2, t=NT)
        masks = carver(cst[:, 2 * P:])
        r_tmp = [masks(2, P) for _ in range(4)]
        assert 2 * P + 8 * P <= N_FIRST - NFREQ

        er, mt = carver(arena[:, MOE_AT:]), carver(mod[:, 0:4096])
        e_s, e_a = er(2, 256), er(2, 256)
        p_tok, pw_tok = er(NT, P), er(NT, P)
        pwT = mod[:, 4096:4096 + SEQ].rearrange("p (t s) -> p t s", t=NT)
        ye = acc
        ysum = arena[:, 0:W_AT].rearrange("p (t n) -> p t n", t=NT)
        strict, iota = mt(P), mt(P)
        late = mod[:, 0:2 * P]
        rw, rb = mt(KC, NE), mt(NE)
        logit, eq1, eq2, key_, l2 = (mt(NT, NE) for _ in range(5))
        m1, m2, i1, i2, e12, w1, w2 = (mt(NT) for _ in range(7))
        table, pick = mt(6, 2 * NE), mt(6, 2 * NE)
        picked, code, hot, item_no, cnt, over, rank_o = (mt(6), mt(2 * NE), mt(2 * NE), mt(1), mt(NE), mt(NE), mt(NE))
        over_hot, over_id = mt(3, NE), mt(3)

        TWO_PARTS = ("ffn_up", "od_qk")
        units, landed, last_in, before = {}, [0] * RING, [None] * RING, {}
        for i, k in enumerate(stream_units()):
            landed[i % RING] += 32 if k[0] in TWO_PARTS else 16
            units[k] = (i % RING, landed[i % RING])
            before[k] = last_in[i % RING]
            last_in[i % RING] = k
        cond_order = [k for k in stream_units() if k[0] == "cond"]
        partial = [k for k in stream_units() if k[0] in ("ffn_down", "od_out") and (k[0], k[1] + 1) in units]

        part_no, used, split_order = {}, {}, []
        for k in stream_units():
            if k[0] != "cond":
                for j in range(unit_parts(k)):
                    part_no[(*k, j)] = len(split_order)
                    if j < unit_parts(k) - 1:
                        used[(*k, j)] = len(used) + 1
                    split_order.append((*k, j))
        N_PARTS, N_USED = len(split_order), len(used)
        low_mark, n_low = {}, {"w_lo": 0, "w_lo_pool": 0}
        for k in split_order:
            sem = "w_lo_pool" if by_pool(k[:-1], k[-1]) else "w_lo"
            n_low[sem] += 1
            low_mark[k] = (sem, n_low[sem])

        def slot_read(eng, key):
            if key[0] == "cond":
                eng.wait_ge(S["cond_acc"], cond_order.index(key) + 1)
            else:
                marks = dict(low_mark[(*key, j)] for j in range(unit_parts(key)))
                for sem, count in marks.items():
                    eng.wait_ge(S[sem], count)

        def part_read(eng, key):
            unit = key[:-1]
            if key in used:
                eng.wait_ge(S["piece_used"], used[key])
            elif unit in partial:
                eng.wait_ge(S["down_units"], partial.index(unit) + 1)
            else:
                last = [(*unit, i) for i in (3, 1) if (*unit, i) in fills] or [(unit[0], 1, 1)]
                filled(eng, *last[0])

        def part_view(flat, key):
            if key[0] in ("ffn_down", "od_out"):
                return flat
            v = flat.rearrange("p (k n) -> p k n", k=2)
            return v[:, :, 0:256] if key[:2] == ("ev_in", 5) else v

        def slot_part(eng, key):
            _, w = weights(eng, *key[:-1])
            return part_view(w[:, key[-1] * PART:(key[-1] + 1) * PART], key)

        def part_buffer(key, low):
            return part_view(w_part[:, part_no[key] % BUFS, low], key)

        def parts_ahead(key):
            last = part_no[(*key, unit_parts(key) - 1)]
            return last + 1 if key == ("ev_in", 3) else min(last + 1 + BUFS, N_PARTS)

        SLOT_USES = N_UNITS // RING
        assert SLOT_USES * RING == N_UNITS

        BLOCKS = ((0, 0), (1, 0), (1, 1))

        def weights(eng, *key):
            s, count = units[key]
            eng.wait_ge(weights_in[s], count)
            return s, ring[:, s * UNIT:(s + 1) * UNIT]

        def to_fill(pe, *key):
            b, n = fills[key]
            if n:
                pe.wait_ge(bank_free[b], n)
            return banks[b], bank_full[b]

        def filled(eng, *key):
            b, n = fills[key]
            eng.wait_ge(bank_full[b], n + 1)
            return banks[b], bank_free[b]

        def taken(eng, *key):
            b, n = fills[key]
            eng.wait_ge(bank_free[b], n + 1)

        def item_taken(eng, it, *key, ago=0):
            b, n = item_at[key]
            eng.wait_ge(bank_free[b], it * item_uses[b] + (fills_before[b] + n + 1 - ago * item_uses[b]))

        def item_to_fill(pe, it, *key):
            b, n = item_at[key]
            pe.wait_ge(bank_free[b], it * item_uses[b] + (fills_before[b] + n))
            return banks[b], bank_full[b]

        def item_filled(eng, it, *key, ago=0):
            b, n = item_at[key]
            eng.wait_ge(bank_full[b], it * item_uses[b] + (fills_before[b] + n + 1 - ago * item_uses[b]))
            return banks[b], bank_free[b]

        def slot_landed(eng, it, a):
            slot, n = a % RING, a // RING
            eng.wait_ge(weights_in[slot], it * (32 * SLOT_USES) + (landed[slot] + 32 * n + 32))
            return ring[:, slot * UNIT:(slot + 1) * UNIT]

        def split(eng, sem, it, n):
            eng.wait_ge(S[sem], it * (2 * N_UNITS) + ({"w_hi": N_PARTS, "w_lo": n_low["w_lo"]}[sem] + n))

        def piece_read(eng, it, n):
            u, half = n // 2, n % 2
            if n < 0:
                item_filled(eng, it, "down", 1, ago=1)
            elif half == 0:
                eng.wait_ge(S["piece_used"], it * N_UNITS + (N_USED + u + 1))
            elif u < N_UP:
                item_filled(eng, it, "up", u)
            elif u < N_UNITS - 1:
                eng.wait_ge(S["down_units"], it * (N_DOWN - 1) + (len(partial) + u - N_UP + 1))
            else:
                item_filled(eng, it, "down", 1)

        def over_loop(eng, body):
            eng.wait_ge(S["over_ready"], 1)
            count = eng.value_load(over_int[0:1, 3:4], min_val=0, max_val=MAX_OVER)
            with eng.Fori(NE, N_ITEMS) as it:
                with eng.If(it < count + NE):
                    body(it)
                eng.nop()

        block = ctx.enter_context(nc.Block())

        @block.sync
        def _(sp):
            def kpn(w, a, b):
                return w[:, a:b].rearrange("(k p) n -> p k n", p=P)

            def halves(w, i):
                half = w.shape[1] // 2
                return [kpn(w, a + 256 * i, a + 256 * i + 256) for a in (0, half)]

            def source(key):
                kind, i = key[0], key[-1]
                q0 = QKV + GH * GD + 2 * GH
                if kind == "cond":
                    return kpn(cond_w[key[1]], 512 * i, 512 * i + 512)
                if kind == "ev_in":
                    a = 512 * i if i < 4 else q0 + 512 * (i - 4)
                    return kpn(ev_w_in[0], a, min(a + 512, ev_w_in.shape[2]))
                if kind == "ev_out":
                    return kpn(ev_w_out[0], 512 * i, 512 * i + 512)
                if kind == "ffn_up":
                    return halves(ffn_w_up[0], i)
                if kind == "od_qk":
                    return halves(od_w_in[0, :, 0:2 * RH * RK], i)
                if kind in ("od_v", "od_g"):
                    a = 2 * RH * RK + (RH * RV if kind == "od_g" else 0) + RV * i
                    return kpn(od_w_in[0], a, a + 512)
                w = ffn_w_down[0] if kind == "ffn_down" else od_w_out[0]
                return w[512 * i:min(512 * i + 512, w.shape[0])].rearrange("(k p) n -> p k n", p=P)

            def load(s, views):
                to = ring[:, s * UNIT:(s + 1) * UNIT]
                if not isinstance(views, list):
                    views = [views]
                for i, view in enumerate(views):
                    if view.shape[2] == D:
                        part = to.rearrange("p (k n) -> p k n", n=D)[:, 0:view.shape[1]]
                    else:
                        part = to.rearrange("p (k n) -> p k n", k=KC)[:, :, 256 * i:256 * i + view.shape[2]]
                    sp.dma_start(part, view).then_inc(weights_in[s], 16)

            sp.dma_start(c_row, c[0].rearrange("(k p) -> k p", p=P)).then_inc(S["c_in"], 16)
            sp.dma_start(cst[:, 0:2 * P], consts[:, 0:2 * P]).then_inc(S["ident_in"], 16)
            sp.dma_start(bias_rows[0:96], cond_b.rearrange("l (r q) -> (l r) q", q=P)).then_inc(S["bias_in"], 16)
            for key in stream_units():
                s, _ = units[key]
                if before[key]:
                    slot_read(sp, before[key])
                load(s, source(key))

            def expert_unit(e, u, a):
                slot = a % RING
                to = ring[:, slot * UNIT:(slot + 1) * UNIT]
                if u < N_UP:
                    w = moe_w_up[0, e].rearrange("(k p) n -> p k n", p=P)
                    load(slot, [w[:, :, c0 + 256 * u:c0 + 256 * u + 256] for c0 in (0, FFE)])
                else:
                    for half in range(2):
                        r = 512 * (u - N_UP) + 256 * half
                        sp.dma_start(to[:, half * PIECE:(half + 1) * PIECE].rearrange("p (k n) -> p k n", n=D),
                                     moe_w_down[0, e, r:r + 256].rearrange("(k p) n -> p k n", p=P)) \
                            .then_inc(weights_in[slot], 16)

            for a in range(RING):
                slot_read(sp, last_in[a])
                expert_unit(0, a, a)
            for a in range(RING, N_UNITS + 1):
                split(sp, "w_lo", 0, 2 * (a - RING) + 2)
                expert_unit(a // N_UNITS, a % N_UNITS, a)
            with sp.Fori(1, NE) as it:
                for a in range(1, N_UNITS + 1):
                    split(sp, "w_lo", it, 2 * (a - RING) + 2)
                    expert_unit(it if a < N_UNITS else (it + 1) % NE, a % N_UNITS, a)

            def over_item(it):
                e = sp.value_load(over_int[0:1, bass.ds(it - NE, 1)], min_val=0, max_val=NE - 1)
                for u in range(N_UNITS):
                    split(sp, "w_lo", it, 2 * (u + 1 - RING) + 2)
                    expert_unit(e, u, u + 1)

            over_loop(sp, over_item)
            for t in range(NT):
                sp.wait_ge(S["ln_done"], 3 * NT + t + 1)
                sp.dma_start(out[0, t * P:(t + 1) * P, :], xs[:, t]).then_inc(S["out_done"], 16)
            sp.wait_ge(S["out_done"], 16 * NT)

        @block.tensor
        def _(pe):
            mm = nc.tensor.matmul
            pe.wait_ge(S["ident_in"], 16)
            pe.wait_ge(S["c_act"], 1)
            bank, full = to_fill(pe, "cT")
            nc.tensor.transpose(bank[:, 0:KC], c_row, ident[0:KC, 0:KC]).then_inc(full, 1)
            cond_n = [0]

            def cond(l, u):
                i = cond_n[0]
                cond_n[0] += 1
                bank, full = to_fill(pe, "cond", l, u)
                pe.wait_ge(S["cond_acc"], i + 1)
                mm(bank[:], ones, acc[:, i % 2], start=True, stop=True).then_inc(full, 1)

            def three(bank, lhs, rhs, start, stop):
                mm(bank, lhs[0], rhs[1], start=start, stop=False)
                mm(bank, lhs[1], rhs[0], start=False, stop=False)
                return mm(bank, lhs[0], rhs[0], start=False, stop=stop)

            def turn(stage, waits, order=(0, 1, 2, 3)):
                for i in order:
                    half, t = i // 2, i % 2
                    waits(half, t)
                    bank, full = to_fill(pe, "hT", stage, i)
                    for j in range(4):
                        k = 4 * half + j
                        last = nc.tensor.transpose(bank[:, j * P:(j + 1) * P], hs[:, t, k * P:(k + 1) * P], ident)
                    last.then_inc(full, 1)

            def h_ready(n):
                return lambda half, t: pe.wait_ge(S["h_ready"], 4 * n + 2 * half + t + 1)

            def part(*key):
                sem, count = low_mark[key]
                pe.wait_ge(S[sem], count)
                return [part_buffer(key, i) for i in range(2)]

            def project(key, stage, n=512):
                for j in range(4):
                    w = part(*key, j)
                    if j == 0:
                        outs = [to_fill(pe, *key, t) for t in range(NT)]
                    for t in range(NT):
                        taken(pe, "hT", stage, j // 2 * 2 + t)
                        bank, full = outs[t]
                        for k in range(2):
                            kk = 2 * j + k
                            last = three(bank[:, 0:n], [a[:, kk, t * P:(t + 1) * P] for a in (hT_hi, hT_lo)],
                                         [a[:, k] for a in w], kk == 0, kk == KC - 1)
                        if j == 3:
                            last.then_inc(full, 1)
                    if j < 3:
                        last.then_inc(S["piece_used"], 1)

            def narrow(region, t):
                for k in range(KC):
                    last = three(region, [a[:, k, t * P:(t + 1) * P] for a in (hT_hi, hT_lo)],
                                 (nw_hi[:, k], nw_lo[:, k]), k == 0, k == KC - 1)
                return last

            for u in FIRST_COND:
                cond(0, u)
            pe.wait_ge(S["convw_in"], 16)
            bank, full = to_fill(pe, "convT")
            nc.tensor.transpose(bank[:, 0:48], conv_rows, ident[0:48, 0:48]).then_inc(full, 1)
            turn(0, h_ready(0))
            pe.wait_ge(S["nw_lo"], 1)
            for t in range(NT):
                for half in range(2):
                    taken(pe, "hT", 0, 2 * half + t)
                bank, full = to_fill(pe, "ab", t)
                narrow(bank[:, 0:8], t).then_inc(full, 1)
            for u in range(3):
                outs = [to_fill(pe, "ev_in", u, i) for i in range(4)]
                for j in range(4):
                    w = part("ev_in", u, j)
                    for i, (bank, full) in enumerate(outs):
                        for k in range(2):
                            kk = 2 * j + k
                            last = three(bank[:, 0:SEQ], [a[:, k, i * P:(i + 1) * P] for a in w],
                                         [a[:, kk] for a in (hT_hi, hT_lo)], kk == 0, kk == KC - 1)
                        if j == 3:
                            last.then_inc(full, 1)
                    if j < 3:
                        last.then_inc(S["piece_used"], 1)
            project(("ev_in", 5), 0, 256)
            project(("ev_in", 4), 0)
            project(("ev_in", 3), 0)
            pe.wait_ge(S["squared"], 1)
            for i in range(4):
                bank, full = to_fill(pe, "l2", i)
                mm(bank[:], ones, norm[:, 512 * i:512 * i + 512], start=True, stop=True).then_inc(full, 1)
            pe.wait_ge(S["g_rhs"], 1)
            for t in range(NT):
                bank, full = to_fill(pe, "g_row", t)
                mm(bank[:], ones, g_rhs[:, GH * t:GH * t + GH], start=True, stop=True).then_inc(full, 1)
            pe.wait_ge(S["b_rhs"], 1)
            for t in range(NT):
                bank, full = to_fill(pe, "b_row", t)
                mm(bank[:], ones, b_rhs[:, GH * t:GH * t + GH], start=True, stop=True).then_inc(full, 1)
            bank, full = to_fill(pe, "g_after")
            mm(bank[:, 0:NTH], cpart["after"], g_tok, start=True, stop=True).then_inc(full, 1)
            pe.wait_ge(S["qk_norm"], 4)
            for name, block_of, ready in (("k_tok", kT, "k_act"), ("v_tok", vT, "v_act")):
                pe.wait_ge(S[ready], 1)
                for t in range(NT):
                    bank, full = to_fill(pe, name, t)
                    for h in range(GH):
                        last = nc.tensor.transpose(bank[:, h * P:(h + 1) * P], block_of(t, h), ident)
                    last.then_inc(full, 1)
            for name, other in (("kk", lambda t, h: kbT[:, GH * t + h]), ("qk", qT)):
                for t in range(NT):
                    if name == "kk":
                        taken(pe, "b_row", t)
                    bank, full = to_fill(pe, name, t)
                    for h in range(GH):
                        last = mm(bank[:, h * P:(h + 1) * P], kT(t, h), other(t, h), start=True, stop=True)
                    last.then_inc(full, 1)
            for t in range(NT):
                pe.wait_ge(S["y0_ready"], t + 1)
                bank, full = to_fill(pe, "xt", t)
                for h in range(GH):
                    last = nc.tensor.transpose(bank[:, h * P:(h + 1) * P], Y[:, GH * t + h], ident)
                last.then_inc(full, 1)
            pe.wait_ge(S["rope_done"], 2)
            for t in range(NT):
                bank, full = to_fill(pe, "att_T", t)
                for g in range(SG):
                    last = nc.tensor.transpose(
                        bank[:, g * P:(g + 1) * P],
                        att_qk[:, t, 2 * g:2 * g + 2].rearrange("p h d -> p (h d)"), ident)
                last.then_inc(full, 1)
            bank, full = to_fill(pe, "att_T", 2)
            for t in range(NT):
                last = nc.tensor.transpose(
                    bank[:, t * P:(t + 1) * P], att_qk[:, t, SH:SH + SKV].rearrange("p h d -> p (h d)"), ident)
            last.then_inc(full, 1)
            def products(key, lhs, rhs):
                bank, full = to_fill(pe, *key)
                t = key[-1]
                for h in range(GH):
                    n = GH * t + h
                    last = mm(bank[:, h * P:(h + 1) * P], lhs[:, n], rhs[:, n], start=True, stop=True)
                last.then_inc(full, 1)

            def attention_scores():
                for i in range(3):
                    taken(pe, "att_T", i)
                for b, (tq, tk) in enumerate(BLOCKS):
                    for v in range(SKV):
                        bank, full = to_fill(pe, "score", b, v)
                        rows = slice(SD * v, SD * v + SD)
                        for g in range(SG):
                            last = mm(bank[:, g * P:(g + 1) * P], att_qT[rows, tq, g], att_kT[rows, tk],
                                      start=True, stop=True)
                        last.then_inc(full, 1)

            for l in range(1, N_LEVELS):
                for t in range(NT):
                    pe.wait_ge(S["level_mask"], 2 * l + t + 1)
                    if l == 1:
                        taken(pe, "xt", t)
                    else:
                        taken(pe, "xax", l - 1, t)
                    products(("ax", l, t), amasks[l % 2], X)
                if l == 1:
                    attention_scores()
                else:
                    cond(0, 2 + l)
                for name in ("xax", "yay") if l < N_LEVELS - 1 else ("yay",):
                    for t in range(NT):
                        taken(pe, "ax", l, t)
                        if l > 1:
                            taken(pe, "yay", l - 1, t)
                        products((name, l, t), *((Y, AXs) if name == "xax" else (AXs, Y)))
            for t in range(NT):
                taken(pe, "v_tok", t)
                taken(pe, "yay", N_LEVELS - 1, t)
                products(("u", t), Y, vb)
            for t in range(NT):
                taken(pe, "k_tok", t)
                products(("w", t), kbg, Y)
            cond(0, 8)
            for b in range(3):
                pe.wait_ge(S["prob_exp"], b + 1)
                for v in range(SKV):
                    bank, full = to_fill(pe, "prob_T", b, v)
                    for g in range(SG):
                        last = nc.tensor.transpose(bank[:, g * P:(g + 1) * P], scores[:, b, SG * v + g], ident)
                    last.then_inc(full, 1)
            for t in range(NT):
                mine = [b for b, (tq, _) in enumerate(BLOCKS) if tq == t]
                for b in mine:
                    for v in range(SKV):
                        taken(pe, "prob_T", b, v)
                bank, full = to_fill(pe, "pv", t)
                for h in range(SH):
                    for b in mine:
                        last = mm(bank[:, h * SD:(h + 1) * SD], pT[b][:, h],
                                  att_v[:, BLOCKS[b][1], (h // SG) * SD:(h // SG + 1) * SD],
                                  start=(b == mine[0]), stop=(b == mine[-1]))
                last.then_inc(full, 1)
            cond(0, 9)

            def v_ready(eng, n):
                if n:
                    taken(eng, "ws", n)
                else:
                    eng.wait_ge(S["v_first"], 1)

            for n in range(4):
                t, rows = n // 2, slice(CHUNK * (n % 2), CHUNK * (n % 2) + CHUNK)
                if n:
                    taken(pe, "w", t)
                    taken(pe, "kv", n - 1)
                    bank, full = to_fill(pe, "ws", n)
                    for h in range(GH):
                        last = mm(bank[:, h * P:(h + 1) * P], wT[:, GH * t + h], state[:, n, h], start=True, stop=True)
                    last.then_inc(full, 1)
                if n < 3:
                    v_ready(pe, n)
                    bank, full = to_fill(pe, "kv", n)
                    for h in range(GH):
                        last = mm(bank[:, h * P:(h + 1) * P], kdec[rows, GH * t + h], vn[rows, GH * t + h],
                                  start=True, stop=True)
                    last.then_inc(full, 1)
            pe.wait_ge(S["q_dec"], 2)
            for t in range(NT):
                v_ready(pe, 2 * t + 1)
                taken(pe, "kv", 2 * t)
                taken(pe, "qk", t)
                bank, full = to_fill(pe, "go", t)
                for h in range(GH):
                    for c_ in range(2):
                        n, rows = 2 * t + c_, slice(CHUNK * c_, CHUNK * c_ + CHUNK)
                        if n:
                            mm(bank[rows, h * P:(h + 1) * P], qdT[:, GH * t + h, rows], state[:, n, h],
                               start=True, stop=False)
                        last = mm(bank[rows, h * P:(h + 1) * P], qkT[:, GH * t + h, rows], vn[:, GH * t + h],
                                  start=not n, stop=True)
                last.then_inc(full, 1)
            turn(1, lambda half, t: taken(pe, "pv", t) if half else pe.wait_ge(S["mix_ready"], t + 1), (2, 3, 0, 1))
            project(("ev_out", 0), 1)
            project(("ev_out", 1), 1)
            turn(2, h_ready(1))

            def down(kind, lhs, n_units, n_chunks, between):
                outs = {(t, h): to_fill(pe, kind, t, h) for t in range(NT) for h in range(2)}
                for i in range(n_units):
                    between(i)
                    parts = unit_parts((kind, i))
                    for j in range(parts):
                        w = part(kind, i, j)
                        ch = 4 * i + j
                        for (t, h), (bank, full) in outs.items():
                            last = three(bank[:], [a[:, ch, t * P:(t + 1) * P] for a in lhs],
                                         [a[:, h * 512:(h + 1) * 512] for a in w], ch == 0, ch == n_chunks - 1)
                            if ch == n_chunks - 1:
                                last.then_inc(full, 1)
                        if j < parts - 1:
                            last.then_inc(S["piece_used"], 1)
                        elif i < n_units - 1:
                            last.then_inc(S["down_units"], 1)

            def ffn_turn(u):
                for t in range(NT):
                    taken(pe, "ffn_up", u, t)
                bank, full = to_fill(pe, "ffn_T", u)
                for j in range(2):
                    for t in range(NT):
                        last = nc.tensor.transpose(bank[:, (2 * j + t) * P:(2 * j + t + 1) * P],
                                                   ff_a[:, u % 2, t, j * P:(j + 1) * P], ident)
                last.then_inc(full, 1)

            for u in range(FFN // 256):
                project(("ffn_up", u), 2)
                if u - 1 in UP_COND:
                    cond(*UP_COND[u - 1])
                if u:
                    ffn_turn(u - 1)

            def ffn_between(i):
                if i == 1:
                    ffn_turn(FFN // 256 - 1)
                if i > 1 and i - 2 in DOWN_COND:
                    cond(*DOWN_COND[i - 2])
                taken(pe, "ffn_T", min(2 * i + 1, FFN // 256 - 1))

            down("ffn_down", (ffT_hi, ffT_lo), 6, FFN // P, ffn_between)
            turn(3, h_ready(2))
            def weighted_values(g):
                taken(pe, "ret_s", g)
                for t in range(NT):
                    taken(pe, "od_v", g, t)
                for t in range(NT):
                    bank, full = to_fill(pe, "ret_y", g, t)
                    for j in range(t + 1):
                        b0 = (0, P, 2 * P)[t + j]
                        last = mm(bank[:], r_s[:, b0:b0 + P], r_v[:, g % 2, j], start=(j == 0), stop=(j == t))
                    last.then_inc(full, 1)

            def turn_rows(g):
                for t in range(NT):
                    pe.wait_ge(S["ret_y"], 2 * g + t + 1)
                    bank, full = to_fill(pe, "ret_yT", g, t)
                    for a in range(4):
                        last = nc.tensor.transpose(bank[:, a * P:(a + 1) * P], r_y[:, t, a * P:(a + 1) * P], ident)
                    last.then_inc(full, 1)

            for h in range(RH):
                project(("od_qk", h), 3)
                if h:
                    cond(1, OD_COND[h - 1])
                    weighted_values(h - 1)
                project(("od_v", h), 3)
                for t in range(NT):
                    pe.wait_ge(S["od_rope"], 2 * h + t + 1)
                    bank, full = to_fill(pe, "ret_T", h, t)
                    for a in range(4):
                        last = nc.tensor.transpose(bank[:, a * P:(a + 1) * P],
                                                   r_qk[:, t, a // 2, (a % 2) * P:(a % 2 + 1) * P], ident)
                    last.then_inc(full, 1)
                project(("od_g", h), 3)
                for t in range(NT):
                    taken(pe, "ret_T", h, t)
                bank, full = to_fill(pe, "ret_s", h)
                for j, q0 in ((0, 0), (1, P)):
                    for a in range(2):
                        last = mm(bank[:, j * SEQ:j * SEQ + SEQ - q0], r_qT[:, 2 + a, j * P:(j + 1) * P],
                                  r_qT[:, a, q0:SEQ], start=(a == 0), stop=(a == 1))
                last.then_inc(full, 1)
                if h:
                    turn_rows(h - 1)
            cond(1, OD_COND[RH - 1])

            def od_between(i):
                if i == 1:
                    weighted_values(RH - 1)
                if i == 2:
                    turn_rows(RH - 1)
                for t in range(NT):
                    taken(pe, "ret_yT", i, t)

            down("od_out", (yT_hi, yT_lo), 4, RH * RV // P, od_between)
            turn(4, h_ready(3))
            pe.wait_ge(S["nw_lo"], 2)
            for i in range(4):
                taken(pe, "hT", 4, i)
            bank, full = to_fill(pe, "router")
            for t in range(NT):
                last = narrow(bank[:, t * NE:(t + 1) * NE], t)
            last.then_inc(full, 1)
            pe.wait_ge(S["late_in"], 16)
            pe.wait_ge(S["rank_in"], 1)
            bank, full = to_fill(pe, "rank")
            mask = [table[:, 2 + t, 0:NE] for t in range(NT)]
            mm(bank[:, 0:NE], strict, mask[0], start=True, stop=True)
            mm(bank[:, NE:2 * NE], strict, mask[1], start=True, stop=False)
            mm(bank[:, NE:2 * NE], ones, mask[0], start=False, stop=True)
            mm(bank[:, 2 * NE:3 * NE], ones, mask[0], start=True, stop=False)
            mm(bank[:, 2 * NE:3 * NE], ones, mask[1], start=False, stop=True).then_inc(full, 1)

            def gather(fill):
                for half in range(2):
                    bank, full = fill(half)
                    for j in range(4):
                        k = 4 * half + j
                        for t in range(NT):
                            last = mm(bank[:, j * P:(j + 1) * P], hs[:, t, k * P:(k + 1) * P], p_tok[:, t],
                                      start=(t == 0), stop=(t == NT - 1))
                    last.then_inc(full, 1)

            pe.wait_ge(S["p_ready"], 1)
            gather(lambda half: to_fill(pe, "gather", half))

            def back(it):
                for h in range(2):
                    item_taken(pe, it, "down", h, ago=1)
                for i in range(4):
                    bank, full = item_to_fill(pe, it, "back", i)
                    mm(bank[:], pwT[:, i // 2], ye[:, i % 2], start=True, stop=True).then_inc(full, 1)

            def item(it, late=0):
                def act_turn(u):
                    item_taken(pe, it, "up", u)
                    bank, full = item_to_fill(pe, it, "act_T", u)
                    for j in range(2):
                        last = nc.tensor.transpose(bank[:, j * P:(j + 1) * P], e_a[:, u % 2, j * P:(j + 1) * P], ident)
                    last.then_inc(full, 1)

                def piece(u, half, view):
                    n = 2 * (u + late) + half
                    split(pe, "w_lo", it, n + 1)
                    return [view(a[:, n % 3]) for a in (w_hi, w_lo)]

                for u in range(N_UP):
                    bank, full = item_to_fill(pe, it, "up", u)
                    for half in range(2):
                        w = piece(u, half, lambda a: a.rearrange("p (k n) -> p k n", k=KC // 2))
                        for k in range(KC // 2):
                            kk = KC // 2 * half + k
                            last = three(bank[:], (heT_hi[:, kk], heT_lo[:, kk]), [a[:, k] for a in w],
                                         kk == 0, kk == KC - 1)
                        last.then_inc(full if half else S["piece_used"], 1)
                        if half == 0 and u:
                            act_turn(u - 1)
                    if u == 0:
                        back(it)
                        pe.wait_ge(S["p_ready"], it + 1)
                        bank, full = item_to_fill(pe, it, "pwT")
                        for t in range(NT):
                            last = nc.tensor.transpose(bank[:, t * P:(t + 1) * P], pw_tok[:, t], ident)
                        last.then_inc(full, 1)
                outs = [item_to_fill(pe, it, "down", h) for h in range(2)]
                for i in range(N_DOWN):
                    for u in (2 * i, 2 * i + 1):
                        item_taken(pe, it, "act_T", u)
                    for half in range(2):
                        w = piece(N_UP + i, half, lambda a: a.rearrange("p (k n) -> p k n", n=D))
                        for h, (bank, full) in enumerate(outs):
                            for k in range(2):
                                ch = 4 * i + 2 * half + k
                                last = three(bank[:], (eT_hi[:, ch], eT_lo[:, ch]),
                                             [a[:, k, h * 512:(h + 1) * 512] for a in w],
                                             ch == 0, ch == 4 * N_DOWN - 1)
                            if half and i == N_DOWN - 1:
                                last.then_inc(full, 1)
                        if half == 0:
                            last.then_inc(S["piece_used"], 1)
                            if i == 0:
                                act_turn(N_UP - 1)
                            if i == 1:
                                pe.wait_ge(S["p_ready"], it + 2)
                                gather(lambda part: item_to_fill(pe, it, "gather", part))
                        elif i < N_DOWN - 1:
                            last.then_inc(S["down_units"], 1)
                for half in range(2):
                    item_taken(pe, it, "gather", half)

            for half in range(2):
                taken(pe, "gather", half)
            pe.wait_ge(S["back_zero"], 2)
            with pe.Fori(0, NE) as it:
                item(it)
            over_loop(pe, lambda it: item(it, 1))
            pe.wait_ge(S["over_ready"], 1)
            back(pe.value_load(over_int[0:1, 3:4], min_val=0, max_val=MAX_OVER) + NE)

        @block.scalar
        def _(act):
            f = nc.scalar.activation
            act.dma_start(posi[:], positions[0].rearrange("(t p) -> p t", p=P),
                          allow_slow_non_contiguous=True).then_inc(S["positions_in"], 16)
            act.dma_start(cst[:, 2 * P:], consts[:, 2 * P:N_FIRST]).then_inc(S["consts_in"], 16)
            act.dma_start(xs[:], x[0].rearrange("(t p) d -> p t d", p=P)).then_inc(S["x_in"], 16)
            act.dma_start(conv_rows, ev_conv_w[0].rearrange("j (c p) -> (j c) p", p=P)).then_inc(S["convw_in"], 16)
            act.dma_start(ab_w, ev_w_in[0, :, QKV + GH * GD:QKV + GH * GD + 2 * GH]
                          .rearrange("(k p) n -> p k n", p=P)).then_inc(S["abw_in"], 16)
            act.wait_ge(S["c_in"], 16)
            f(c_row, c_row, ACT.Silu).then_inc(S["c_act"], 1)

            def cond(l, u):
                if l == 1:
                    if u < 10:
                        act.wait_ge(S["h_ready"], 8)
                    else:
                        act.wait_ge(S["ln_done"], 4)
                bank, free = filled(act, "cond", l, u)
                scale = 1.0 if u // 2 in (1, 4) else 0.0
                f(mod[:, 512 * u:512 * u + 512], bank[:], ACT.Copy, bias=scale).then_inc(free, 1)

            def copy(key, to, view=None, func=ACT.Copy, scale=1.0):
                bank, free = filled(act, *key)
                src = bank[:] if view is None else view(bank)
                f(to, src, func, scale=scale).then_inc(free, 1)

            def turned(stage, order=(0, 1, 2, 3)):
                for i in order:
                    half, t = i // 2, i % 2
                    bank, _ = filled(act, "hT", stage, i)
                    f(hT_hi[:, 4 * half:4 * half + 4, t * P:(t + 1) * P], bank[:].rearrange("p (k s) -> p k s", k=4),
                      ACT.Copy).then_inc(S["turn_hi"], 1)

            at = [0]

            def split_to(end):
                for key in split_order[at[0]:end]:
                    n = part_no[key]
                    if n >= BUFS:
                        part_read(act, split_order[n - BUFS])
                    f(part_buffer(key, 0), slot_part(act, key), ACT.Copy).then_inc(S["w_hi"], 1)
                at[0] = max(at[0], end)

            def split_ahead(*key):
                split_to(parts_ahead(key))

            heads = lambda b: b[:].rearrange("p (h j) -> p h j", h=GH)

            act.wait_ge(S["abw_in"], 16)
            f(nw_hi[:], ab_w, ACT.Copy).then_inc(S["nw_hi"], 1)
            for u in FIRST_COND:
                cond(0, u)
            for i in range(2):
                act.wait_ge(S["angle_ready"], i + 1)
                f(trig[:, i], ang[i], ACT.Sin).then_inc(S["trig_ready"], 1)
            turned(0)
            split_to(BUFS)
            for t in range(NT):
                copy(("ab", t), ab[:, t], lambda b: b[:, 0:8])
            act.wait_ge(S["pads_zero"], 1)
            for u in range(3):
                split_ahead("ev_in", u)
                for i in range(4):
                    copy(("ev_in", u, i), conv_x[:, 4 * u + i, CONV_W - 1:], lambda b: b[:, 0:SEQ])
            split_ahead("ev_in", 5)
            for t in range(NT):
                bank, free = filled(act, "ev_in", 5, t)
                f(att_qk[:, t, SH:], bank[:, 0:P].rearrange("p (h d) -> p h d", h=SKV), ACT.Copy).then_inc(S["k_raw"], 1)
                f(att_v[:, t], bank[:, P:2 * P], ACT.Copy).then_inc(free, 1)
            split_ahead("ev_in", 4)
            for t in range(NT):
                copy(("ev_in", 4, t), att_qk[:, t, 0:SH].rearrange("p (g v) d -> p g v d", v=SKV),
                     lambda b: b[:].rearrange("p (v g d) -> p g v d", v=SKV, g=SG))
            act.wait_ge(S["gates_in"], 32)
            act.wait_ge(S["gate_in"], 2)
            f(g_a, g_a, ACT.Exp, scale=-1.0).then_inc(S["gate_exp"], 1)
            f(g_b, g_b, ACT.Exp).then_inc(S["gate_exp"], 1)
            f(alog, alog, ACT.Exp).then_inc(S["gate_exp"], 1)
            act.wait_ge(S["h_ready"], 4)
            split_ahead("ev_in", 3)
            for t in range(NT):
                copy(("ev_in", 3, t), zs[:, t], func=ACT.Silu)
            for name, lo in (("q_act", 0), ("k_act", GH), ("v_act", 2 * GH)):
                act.wait_ge(S["conv_done"], lo // GH + 1)
                f(conv_y[:, lo:lo + GH], conv_y[:, lo:lo + GH], ACT.Silu).then_inc(S[name], 1)
            for i, name in enumerate(("q_act", "k_act")):
                act.wait_ge(S[name], 1)
                last = f(norm[:, 1024 * i:1024 * i + 1024].rearrange("p (c t) -> p c t", c=GH),
                         conv_y[:, GH * i:GH * i + GH], ACT.Square)
            last.then_inc(S["squared"], 1)
            for i in range(4):
                bank, free = filled(act, "l2", i)
                f(norm[:, 512 * i:512 * i + 512], bank[:], ACT.Sqrt, bias=eps_n).then_inc(free, 1)
            for t in range(NT):
                bank, _ = filled(act, "g_row", t)
                f(eG[:, GH * t:GH * t + GH], heads(bank), ACT.Exp).then_inc(S["exp_row"], 1)
            copy(("g_after",), e_after, lambda b: b[:, 0:NTH], ACT.Exp)
            for t in range(NT):
                taken(act, "g_row", t)
                f(dec[:, GH * t:GH * t + GH], dec[:, GH * t:GH * t + GH], ACT.Exp).then_inc(S["dec_exp"], 1)
            f(e_col, g_col, ACT.Exp).then_inc(S["e_col"], 1)
            for t in range(NT):
                copy(("xt", t), X[:, GH * t:GH * t + GH], heads)
            for t in range(NT):
                copy(("att_T", t), att_qT[:, t], heads)
            copy(("att_T", 2), att_kT, lambda b: b[:, 0:NT * P].rearrange("p (t j) -> p t j", t=NT))
            for l in range(1, N_LEVELS):
                for t in range(NT):
                    copy(("ax", l, t), AXs[:, GH * t:GH * t + GH], heads)
                if l > 1:
                    cond(0, 2 + l)
                if l > 2:
                    b = l - 3
                    act.wait_ge(S["score_sub"], b + 1)
                    f(scores[:, b], scores[:, b], ACT.Exp).then_inc(S["prob_exp"], 1)
            act.wait_ge(S["sink_sub"], 1)
            f(es, es, ACT.Exp).then_inc(S["sink_exp"], 1)
            for t in range(NT):
                copy(("u", t), U[:, GH * t:GH * t + GH], heads)
            for t in range(NT):
                copy(("w", t), wT[:, GH * t:GH * t + GH], heads)
            cond(0, 8)
            for b in range(3):
                for v in range(SKV):
                    copy(("prob_T", b, v), pT[b][:, SG * v:SG * v + SG], heads)
            cond(0, 9)
            for t in range(NT):
                copy(("go", t), o_tok[:, GH * t:GH * t + GH], heads)
            for t in range(NT):
                act.wait_ge(S["ssq_ready"], t + 1)
                f(rstd_o[:, GH * t:GH * t + GH], ssq[:, GH * t:GH * t + GH], ACT.Sqrt, bias=eps_n,
                  scale=1.0 / GD).then_inc(S["o_rstd"], 1)

            def deviations(var_ready, done, first, eps):
                for t in range(NT):
                    act.wait_ge(S[var_ready], first + t + 1)
                    f(rstd[:, t:t + 1], aggr[:, t, 1:2], ACT.Sqrt, bias=eps).then_inc(S[done], 1)

            turned(1, (2, 3, 0, 1))
            split_to(part_no["ev_out", 0, 0] + BUFS)
            for u in range(2):
                split_ahead("ev_out", u)
            deviations("resid_var", "resid_rstd", 0, eps_ln)
            turned(2)

            def ffn_turned(u):
                bank, _ = filled(act, "ffn_T", u)
                f(ffT_hi[:, 2 * u:2 * u + 2], bank[:].rearrange("p (j s) -> p j s", j=2), ACT.Copy) \
                    .then_inc(S["rows_hi"], 1)

            for u in range(FFN // 256):
                split_ahead("ffn_up", u)
                for t in range(NT):
                    if u >= 2:
                        taken(act, "ffn_up", u - 2, t)
                    bank, _ = filled(act, "ffn_up", u, t)
                    f(ff_s[:, u % 2, t], bank[:, 0:256], ACT.Silu).then_inc(S["ffn_silu"], 1)
                if u - 1 in UP_COND:
                    cond(*UP_COND[u - 1])
                if u:
                    ffn_turned(u - 1)
            for i in range(6):
                if i > 1 and i - 2 in DOWN_COND:
                    cond(*DOWN_COND[i - 2])
                split_ahead("ffn_down", i)
                if i == 0:
                    ffn_turned(FFN // 256 - 1)
            deviations("resid_var", "resid_rstd", NT, eps_ln)
            turned(3)

            def turned_rows(g):
                for t in range(NT):
                    bank, _ = filled(act, "ret_yT", g, t)
                    f(yT_hi[:, 4 * g:4 * g + 4, t * P:(t + 1) * P], heads(bank), ACT.Copy).then_inc(S["rows_hi"], 1)

            for h in range(RH):
                split_ahead("od_qk", h)
                if h:
                    cond(1, OD_COND[h - 1])
                    deviations("ret_var", "ret_rstd", NT * (h - 1), eps_n)
                split_ahead("od_v", h)
                for t in range(NT):
                    if h >= 2:
                        filled(act, "ret_y", h - 2, NT - 1)
                    copy(("od_v", h, t), r_v[:, h % 2, t])
                for t in range(NT):
                    copy(("ret_T", h, t), r_qT[:, :, t * P:(t + 1) * P], heads)
                split_ahead("od_g", h)
                for t in range(NT):
                    if h >= 2:
                        act.wait_ge(S["ret_y"], 2 * (h - 2) + NT)
                    copy(("od_g", h, t), r_g[:, h % 2, t], func=ACT.Silu)
                if h:
                    turned_rows(h - 1)
            cond(1, OD_COND[RH - 1])
            for i in range(4):
                split_ahead("od_out", i)
                if i == 0:
                    deviations("ret_var", "ret_rstd", NT * (RH - 1), eps_n)
                if i == 1:
                    turned_rows(RH - 1)
            act.wait_ge(S["router_in"], 32)
            f(nw_hi[:], rw, ACT.Copy).then_inc(S["nw_hi"], 1)
            filled(act, "od_out", 1, 1)
            w = slot_landed(act, 0, 0)
            for half in range(2):
                f(w_hi[:, half], w[:, half * PIECE:(half + 1) * PIECE], ACT.Copy).then_inc(S["w_hi"], 1)
            deviations("resid_var", "resid_rstd", 2 * NT, eps_ln)
            turned(4)
            act.wait_ge(S["route_in"], 1)
            f(e12, e12, ACT.Exp).then_inc(S["route_exp"], 1)
            for half in range(2):
                bank, _ = filled(act, "gather", half)
                f(heT_hi[:, 4 * half:4 * half + 4], heads(bank), ACT.Copy).then_inc(S["tok_hi"], 1)

            def item(it, late=0):
                def take(key, to, view, func=ACT.Copy):
                    bank, free = item_filled(act, it, *key)
                    f(to, view(bank), func).then_inc(free, 1)

                def split_unit(u):
                    w = slot_landed(act, it, u + late)
                    for half in range(2):
                        n = 2 * u + half
                        piece_read(act, it, n - 3)
                        f(w_hi[:, (n + 2 * late) % 3], w[:, half * PIECE:(half + 1) * PIECE], ACT.Copy) \
                            .then_inc(S["w_hi"], 1)

                if late:
                    split(act, "w_lo", it, 2)
                    split_unit(0)
                for u in range(N_UNITS):
                    if 1 <= u <= N_UP:
                        item_taken(act, it, "up", (u - 3) % N_UP, ago=int(u < 3))
                        bank, _ = item_filled(act, it, "up", u - 1)
                        f(e_s[:, (u - 1) % 2], bank[:, 0:256], ACT.Silu).then_inc(S["e_silu"], 1)
                    if u < N_UNITS - late:
                        split_unit(u + 1)
                    if u == 0:
                        take(("pwT",), pwT, lambda b: b[:, 0:SEQ].rearrange("p (t s) -> p t s", t=NT))
                    if 1 <= u <= N_UP:
                        bank, _ = item_filled(act, it, "act_T", u - 1)
                        f(eT_hi[:, 2 * u - 2:2 * u], bank[:, 0:256].rearrange("p (j s) -> p j s", j=2),
                          ACT.Copy).then_inc(S["act_hi"], 1)
                    if u == N_UP + 1:
                        for half in range(2):
                            bank, _ = item_filled(act, it, "gather", half)
                            f(heT_hi[:, 4 * half:4 * half + 4], heads(bank), ACT.Copy).then_inc(S["tok_hi"], 1)
                for h in range(2):
                    take(("down", h), ye[:, h], lambda b: b[:])

            with act.Fori(0, NE) as it:
                item(it)
            over_loop(act, lambda it: item(it, 1))
            deviations("resid_var", "resid_rstd", 3 * NT, eps_ln)

        @block.vector
        def _(dve):
            V = Steps(dve, S["dve_step"])
            tt, ts, stt = nc.vector.tensor_tensor, nc.vector.tensor_scalar, nc.vector.scalar_tensor_tensor
            quad = lambda a, t: a[:, GH * t:GH * t + GH]
            heads = lambda b: b[:].rearrange("p (h j) -> p h j", h=GH)

            V.do(nc.vector.memset(eps_n, NORM_EPS))
            V.do(nc.vector.memset(eps_ln, LN_EPS))
            nc.vector.memset(conv_x[:, :, 0:CONV_W - 1], 0.0).then_inc(S["pads_zero"], 1)
            bank, free = filled(dve, "cT")
            nc.vector.tensor_copy(cT, bank[:, 0:KC]).then_inc(free, 1)
            def turns():
                dve.wait_ge(S["consts_in"], 16)
                dve.wait_ge(S["positions_in"], 16)
                V.then(nc.vector.tensor_copy(posf, posi[:]))
                for t in range(NT):
                    V.do(ts(ang[2][:, t], cpart["freq"], posf[:, t:t + 1], None, ALU.mult))
                V.wait()
                V.then(ts(ang[3], ang[2], 1.0 / TWO_PI, ROUND, ALU.mult, ALU.add))
                V.then(ts(ang[3], ang[3], ROUND, None, ALU.subtract))
                for part in (PI2_A, PI2_B, PI2_C):
                    V.then(stt(ang[2], ang[3], -part, ang[2], ALU.mult, ALU.add))
                ts(ang[0], ang[2], PI_MAX, -PI_MAX, ALU.min, ALU.max).then_inc(S["angle_ready"], 1)
                V.then(ts(ang[2], ang[2], TWO_PI / 4, None, ALU.add))
                V.then(ts(ang[3], ang[2], PI_MAX, -TWO_PI, ALU.is_gt, ALU.mult))
                V.then(tt(ang[2], ang[2], ang[3], ALU.add))
                ts(ang[1], ang[2], PI_MAX, -PI_MAX, ALU.min, ALU.max).then_inc(S["angle_ready"], 1)

            cond_n = [0]
            dve.wait_ge(S["bias_in"], 16)
            dve.wait_ge(S["ident_in"], 16)
            taken(dve, "cT")

            def cond(l, u):
                i = cond_n[0]
                cond_n[0] += 1
                to = acc[:, i % 2]
                if i >= 2:
                    filled(dve, *cond_order[i - 2])
                _, w = weights(dve, "cond", l, u)
                w = w.rearrange("p (k n) -> p k n", k=KC)
                V.then(ts(to, w[:, 0], cT[:, 0:1], None, ALU.mult))
                for k in range(1, KC):
                    V.then(stt(to, w[:, k], cT[:, k:k + 1], to, ALU.mult, ALU.add))
                for j in range(4):
                    row = 48 * l + 4 * u + j
                    cols = slice(j * P, (j + 1) * P)
                    last = stt(to[0:96, cols], bias_rows[0:96], ident[0:96, row:row + 1], to[0:96, cols], ALU.mult, ALU.add)
                    if j < 3:
                        V.do(last)
                last.then_inc(S["cond_acc"], 1)

            def modulate(l, shift):
                for half in range(2):
                    taken(dve, "cond", l, 2 * shift + half)
                    taken(dve, "cond", l, 2 * shift + 2 + half)
                    a = shift * D + 512 * half
                    cols = slice(512 * half, 512 * half + 512)
                    for t in range(NT):
                        V.do(tt(hs[:, t, cols], xs[:, t, cols], mod[:, a + D:a + D + 512], ALU.mult))
                    V.wait()
                    for t in range(NT):
                        tt(hs[:, t, cols], hs[:, t, cols], mod[:, a:a + 512], ALU.add).then_inc(S["h_ready"], 1)

            def turned(stage, order=(0, 1, 2, 3)):
                for n, i in enumerate(order):
                    half, t = i // 2, i % 2
                    bank, free = filled(dve, "hT", stage, i)
                    dve.wait_ge(S["turn_hi"], 4 * stage + n + 1)
                    to = (slice(None), slice(4 * half, 4 * half + 4), slice(t * P, (t + 1) * P))
                    tt(hT_lo[to], bank[:].rearrange("p (k s) -> p k s", k=4), hT_hi[to].bitcast(F32),
                       ALU.subtract).then_inc(free, 1)

            at = [0]

            def split_to(end):
                for key in split_order[at[0]:end]:
                    if low_mark[key][0] != "w_lo":
                        continue
                    dve.wait_ge(S["w_hi"], part_no[key] + 1)
                    tt(part_buffer(key, 1), slot_part(dve, key), part_buffer(key, 0).bitcast(F32),
                       ALU.subtract).then_inc(S["w_lo"], 1)
                at[0] = max(at[0], end)

            def split_ahead(*key):
                split_to(parts_ahead(key))

            def rest(it, n, slot, buf):
                split(dve, "w_hi", it, n + 1)
                at = ring[:, slot * UNIT + (n % 2) * PIECE:slot * UNIT + (n % 2 + 1) * PIECE]
                tt(w_lo[:, buf], at, w_hi[:, buf].bitcast(F32), ALU.subtract).then_inc(S["w_lo"], 1)

            rows_n = [0]

            def rows_turned(key, to, view):
                rows_n[0] += 1
                bank, free = filled(dve, *key)
                dve.wait_ge(S["rows_hi"], rows_n[0])
                hi, lo = to
                tt(lo, view(bank), hi.bitcast(F32), ALU.subtract).then_inc(free, 1)

            def residual(l, gate, key, t, half):
                cols = slice(512 * half, 512 * half + 512)
                for u in (2 * gate, 2 * gate + 1):
                    taken(dve, "cond", l, u)
                if key:
                    bank, free = filled(dve, *key)
                    tt(hs[:, t, cols], bank[:], mod[:, gate * D + 512 * half:gate * D + 512 * half + 512],
                       ALU.mult).then_inc(free, 1)
                    taken(dve, *key)
                else:
                    V.then(tt(hs[:, t, cols], ysum[:, t, cols],
                              mod[:, gate * D + 512 * half:gate * D + 512 * half + 512], ALU.mult))
                V.do(stt(hs[:, t, cols], xs[:, t, cols], ALPHA, hs[:, t, cols], ALU.mult, ALU.add))

            def layer_norm(stage):
                V.wait()
                for t in range(NT):
                    for k in range(2):
                        V.do(nc.vector.bn_stats(stats[:, t, k], hs[:, t, 512 * k:512 * k + 512]))
                for t in range(NT):
                    V.wait()
                    nc.vector.bn_aggr(aggr[:, t], stats[:, t]).then_inc(S["resid_var"], 1)
                dve.wait_ge(S["ln_in"], 32 * (stage + 1))
                for t in range(NT):
                    dve.wait_ge(S["resid_rstd"], NT * stage + t + 1)
                    V.then(nc.vector.reciprocal(rstd[:, t:t + 1], rstd[:, t:t + 1]))
                    V.then(ts(hs[:, t], hs[:, t], aggr[:, t, 0:1], rstd[:, t:t + 1], ALU.subtract, ALU.mult))
                    V.then(tt(hs[:, t], hs[:, t], ln[:, 0], ALU.mult))
                    tt(xs[:, t], hs[:, t], ln[:, 1], ALU.add).then_inc(S["ln_done"], 1)
                dve.wait_ge(S["ln_done"], NT * stage + NT)

            def narrow_lo(w, n):
                dve.wait_ge(S["nw_hi"], n)
                tt(nw_lo[:], w, nw_hi[:].bitcast(F32), ALU.subtract).then_inc(S["nw_lo"], 1)

            for n, u in enumerate(FIRST_COND):
                cond(0, u)
                if n == 0:
                    turns()
            narrow_lo(ab_w, 1)
            bank, free = filled(dve, "convT")
            nc.vector.tensor_copy(conv_w, bank[:, 0:48]).then_inc(free, 1)
            dve.wait_ge(S["x_in"], 16)
            modulate(0, 0)
            turned(0)
            split_to(BUFS)
            split_ahead("ev_in", 0)
            for t in range(NT):
                taken(dve, "ab", t)
            dve.wait_ge(S["gates_in"], 32)
            as8 = lambda a: a.rearrange("p (t h) -> p t h", t=NT)
            V.then(tt(as8(g_c), ab[:, :, 0:GH], over_all(dtb, NT), ALU.add))
            stt(g_a, g_c, -1.0, g_c, ALU.mult, ALU.max).then_inc(S["gate_in"], 1)
            ts(as8(g_b), ab[:, :, GH:2 * GH], -1.0, 80.0, ALU.mult, ALU.min).then_inc(S["gate_in"], 1)
            split_ahead("ev_in", 1)
            taken(dve, "convT")
            for i in range(3):
                split_ahead(*(("ev_in", 2), ("ev_in", 5), ("ev_in", 4))[i])
                for u in range(4):
                    taken(dve, "ev_in", i, u)
                for j in range(CONV_W):
                    for ch in range(GH * i, GH * i + GH):
                        w = conv_w[:, j * NF + ch:j * NF + ch + 1]
                        if j == 0:
                            last = ts(conv_y[:, ch], conv_x[:, ch, 0:SEQ], w, None, ALU.mult)
                        else:
                            last = stt(conv_y[:, ch], conv_x[:, ch, j:j + SEQ], w, conv_y[:, ch], ALU.mult, ALU.add)
                        if (j, ch) != (CONV_W - 1, GH * i + GH - 1):
                            V.do(last)
                    if j < CONV_W - 1:
                        V.wait()
                last.then_inc(S["conv_done"], 1)
            split_ahead("ev_in", 3)
            dve.wait_ge(S["gate_exp"], 3)
            V.then(ts(g_b, g_b, 1.0, None, ALU.add))
            V.do(nc.vector.reciprocal(beta, g_b))
            V.then(ts(g_d, g_a, 2.0, None, ALU.add))
            V.then(nc.vector.reciprocal(g_d, g_d))
            V.then(tt(g_a, g_a, g_d, ALU.mult))
            V.then(tt(g_b, g_a, g_a, ALU.mult))
            V.then(ts(g_d, g_b, 1.0 / 17, None, ALU.mult))
            for n in range(15, 1, -2):
                V.then(stt(g_d, g_d, 1.0 / n, g_b, ALU.add, ALU.mult))
            V.then(stt(g_d, g_d, 1.0, g_a, ALU.add, ALU.mult))
            V.then(ts(g_c, g_c, 0.0, None, ALU.max))
            V.then(stt(g_d, g_d, 2.0, g_c, ALU.mult, ALU.add))
            V.then(stt(as8(g_tok), as8(g_d), -1.0, over_all(alog, NT), ALU.mult, ALU.mult))
            dve.wait_ge(S["trig_ready"], 2)
            tt(g_rhs, per_row(g_tok, P), over_all(cpart["upto"], NTH), ALU.mult).then_inc(S["g_rhs"], 1)
            tt(b_rhs, per_row(beta, P), over_all(ident, NTH), ALU.mult).then_inc(S["b_rhs"], 1)
            for i in range(4):
                taken(dve, "l2", i)
                n_i = norm[:, 512 * i:512 * i + 512]
                V.then(nc.vector.reciprocal(n_i, n_i))
                y_i = conv_y[:, 2 * i:2 * i + 2]
                stt(y_i, y_i, GD ** -0.5 if i < 2 else 1.0, n_i.rearrange("p (c t) -> p c t", c=2),
                    ALU.mult, ALU.mult).then_inc(S["qk_norm"], 1)
            dve.wait_ge(S["qk_norm"], 4)
            for t in range(NT):
                taken(dve, "ev_in", 4, t)
                taken(dve, "ev_in", 5, t)
            dve.wait_ge(S["trig_ready"], 2)
            col = lambda a: a[:, :, RK // 2:].unsqueeze(2).broadcast_to([P, NT, SH + SKV, SROT])
            x1, x2 = att_qk[:, :, :, 0:SROT], att_qk[:, :, :, SROT:2 * SROT]
            for to, a, b in ((0, x1, cos_t), (1, x2, sin_t), (2, x2, cos_t), (3, x1, sin_t)):
                V.do(tt(rope_tmp[to], a, col(b), ALU.mult))
            V.wait()
            tt(x1, rope_tmp[0], rope_tmp[1], ALU.subtract).then_inc(S["rope_done"], 1)
            tt(x2, rope_tmp[2], rope_tmp[3], ALU.add).then_inc(S["rope_done"], 1)
            for t in range(NT):
                bank, free = filled(dve, "g_row", t)
                dve.wait_ge(S["exp_row"], t + 1)
                V.then(tt(quad(dec, t), heads(bank), over_all(ident, GH), ALU.mult))
                V.then(nc.vector.tensor_reduce(quad(g_col, t), quad(dec, t), AX.X, ALU.add))
                for h in range(GH):
                    n = GH * t + h
                    last = stt(dec[:, n], bank[:, h * P:(h + 1) * P], g_col[:, n:n + 1], cpart["upto"],
                               ALU.subtract, ALU.mult)
                    if h < GH - 1:
                        V.do(last)
                last.then_inc(free, 1)
            for t in range(NT):
                bank, free = filled(dve, "b_row", t)
                tt(quad(kbT, t), by_tile(GH, t), heads(bank), ALU.mult).then_inc(free, 1)
            for t in range(NT):
                dve.wait_ge(S["dec_exp"], t + 1)
                V.do(tt(quad(dec, t), quad(dec, t), over_all(cpart["upto"], GH), ALU.mult))
            dve.wait_ge(S["e_col"], 1)
            V.then(tt(bg, beta, e_col, ALU.mult))
            taken(dve, "g_after")
            for t in range(NT):
                bank, free = filled(dve, "k_tok", t)
                V.do(tt(quad(kbg, t), heads(bank), per_row(quad(bg, t), P), ALU.mult))
                tt(quad(kdec, t), heads(bank), per_row(quad(e_after, t), P), ALU.mult).then_inc(free, 1)
            for t in range(NT):
                bank, free = filled(dve, "v_tok", t)
                tt(quad(vb, t), heads(bank), per_row(quad(beta, t), P), ALU.mult).then_inc(free, 1)
            for name, to in (("kk", aD), ("qk", qkT)):
                for t in range(NT):
                    if name == "kk":
                        filled(dve, "v_tok", NT - 1)
                    bank, free = filled(dve, name, t)
                    tt(quad(to, t), heads(bank), quad(dec, t), ALU.mult).then_inc(free, 1)
            for t in range(NT):
                dve.wait_ge(S["level_mask"], t + 1)
                tt(quad(Y, t), over_all(ident, GH), quad(amasks[0], t), ALU.subtract).then_inc(S["y0_ready"], 1)

            def block_scores(b):
                mask = cpart["att_prev" if b == 1 else "att_own"]
                for v in range(SKV):
                    bank, free = filled(dve, "score", b, v)
                    stt(scores[:, b, SG * v:SG * v + SG], heads(bank), SD ** -0.5, over_all(mask, SG),
                        ALU.mult, ALU.add).then_inc(free, 1)
                    taken(dve, "score", b, v)
                V.then(nc.vector.tensor_reduce(mx3[:, b], scores[:, b], AX.X, ALU.max))

            def subtract_max(b):
                tt(scores[:, b], scores[:, b], per_row(mx[:, BLOCKS[b][0]], P), ALU.subtract).then_inc(S["score_sub"], 1)

            def attention(l):
                if l == 1:
                    block_scores(2)
                if l == 2:
                    dve.wait_ge(S["sinks_in"], 16)
                    V.do(tt(mx[:, 0], mx3[:, 0], sinks, ALU.max))
                    V.then(tt(mx[:, 1], mx3[:, 1], mx3[:, 2], ALU.max))
                    V.then(tt(mx[:, 1], mx[:, 1], sinks, ALU.max))
                    tt(es, over_all(sinks, NT), mx, ALU.subtract).then_inc(S["sink_sub"], 1)
                    for b in range(3):
                        subtract_max(b)

            block_scores(0)
            block_scores(1)
            for l in range(1, N_LEVELS):
                if l < N_LEVELS - 1:
                    for t in range(NT):
                        bank, free = filled(dve, "xax", l, t)
                        taken(dve, *(("xax", l - 1, t) if l > 1 else ("xt", t)))
                        tt(quad(X, t), quad(X, t), heads(bank), ALU.subtract).then_inc(free, 1)
                for t in range(NT):
                    bank, free = filled(dve, "yay", l, t)
                    if l > 1:
                        taken(dve, "yay", l - 1, t)
                    else:
                        dve.wait_ge(S["y0_ready"], t + 1)
                    tt(quad(Y, t), quad(Y, t), heads(bank), ALU.subtract).then_inc(free, 1)
                attention(l)
                cond(0, 3 + l)
            taken(dve, "u", 0)
            nc.vector.tensor_copy(vn[0:CHUNK, 0:GH], U[0:CHUNK, 0:GH]).then_inc(S["v_first"], 1)
            for b in range(3):
                dve.wait_ge(S["prob_exp"], b + 1)
                V.do(nc.vector.tensor_reduce(sm3[:, b], scores[:, b], AX.X, ALU.add))
            cond(0, 9)
            dve.wait_ge(S["sink_exp"], 1)
            V.wait()
            V.do(tt(es[:, 0], es[:, 0], sm3[:, 0], ALU.add))
            V.then(tt(es[:, 1], es[:, 1], sm3[:, 1], ALU.add))
            V.then(tt(es[:, 1], es[:, 1], sm3[:, 2], ALU.add))
            V.then(nc.vector.reciprocal(es, es))
            for t in range(NT):
                bank, free = filled(dve, "pv", t)
                tt(om[:, t, GH * GD:].rearrange("p (h d) -> p h d", d=SD), bank[:].rearrange("p (h d) -> p h d", d=SD),
                   per_row(es[:, t], SD), ALU.mult).then_inc(free, 1)
            for n in range(4):
                t, rows = n // 2, slice(CHUNK * (n % 2), CHUNK * (n % 2) + CHUNK)
                if n:
                    bank, free = filled(dve, "ws", n)
                    taken(dve, "u", t)
                    tt(quad(vn[rows], t), quad(U[rows], t), heads(bank)[rows], ALU.subtract).then_inc(free, 1)
                if n < 3:
                    bank, free = filled(dve, "kv", n)
                    if n == 0:
                        nc.vector.tensor_copy(state[:, 1], heads(bank)).then_inc(free, 1)
                    else:
                        taken(dve, "kv", n - 1)
                        for h in range(GH):
                            end = rows.stop - 1
                            last = stt(state[:, n + 1, h], state[:, n, h], eG[:, GH * t + h, end:end + 1],
                                       bank[:, h * P:(h + 1) * P], ALU.mult, ALU.add)
                            if h < GH - 1:
                                V.do(last)
                        last.then_inc(free, 1)
            for t in range(NT):
                taken(dve, "go", t)
                V.then(tt(quad(o_sq, t), quad(o_tok, t), quad(o_tok, t), ALU.mult))
                nc.vector.tensor_reduce(quad(ssq, t), quad(o_sq, t), AX.X, ALU.add).then_inc(S["ssq_ready"], 1)
            for t in range(NT):
                taken(dve, "pv", t)
                dve.wait_ge(S["o_rstd"], t + 1)
                V.then(nc.vector.reciprocal(quad(rstd_o, t), quad(rstd_o, t)))
                V.then(tt(quad(o_tok, t), quad(o_tok, t), per_row(quad(rstd_o, t), P), ALU.mult))
                dve.wait_ge(S["z_w"], t + 1)
                tt(om[:, t, 0:GH * GD].rearrange("p (h d) -> p h d", h=GH), quad(o_tok, t),
                   zs[:, t].rearrange("p (h d) -> p h d", h=GH), ALU.mult).then_inc(S["mix_ready"], 1)
            turned(1, (2, 3, 0, 1))
            split_to(part_no["ev_out", 0, 0] + BUFS)
            for u in range(2):
                split_ahead("ev_out", u)
                for t in range(NT):
                    residual(0, 2, ("ev_out", u, t), t, u)
            layer_norm(0)
            modulate(0, 3)
            turned(2)

            def ffn_turned(u):
                rows_turned(("ffn_T", u), [a[:, 2 * u:2 * u + 2] for a in (ffT_hi, ffT_lo)],
                            lambda b: b[:].rearrange("p (j s) -> p j s", j=2))

            for u in range(FFN // 256):
                split_ahead("ffn_up", u)
                for t in range(NT):
                    bank, free = filled(dve, "ffn_up", u, t)
                    dve.wait_ge(S["ffn_silu"], NT * u + t + 1)
                    if u >= 2:
                        filled(dve, "ffn_T", u - 2)
                    tt(ff_a[:, u % 2, t], ff_s[:, u % 2, t], bank[:, 256:512], ALU.mult).then_inc(free, 1)
                if u in UP_COND:
                    cond(*UP_COND[u])
                if u:
                    ffn_turned(u - 1)
            for i in range(6):
                split_ahead("ffn_down", i)
                if i == 0:
                    ffn_turned(FFN // 256 - 1)
                if i in DOWN_COND:
                    cond(*DOWN_COND[i])
            for t in range(NT):
                for half in range(2):
                    residual(0, 5, ("ffn_down", t, half), t, half)
            layer_norm(1)
            modulate(1, 0)
            turned(3)

            def rotate(h):
                for t in range(NT):
                    bank, free = filled(dve, "od_qk", h, t)
                    x1, x2 = (bank[:].rearrange("p (a n) -> p a n", a=2)[:, :, i * P:(i + 1) * P] for i in range(2))
                    tabs = [over_all(a[:, t, 0:P], 2) for a in (cos_t, sin_t)]
                    if NT * h + t:
                        dve.wait_ge(S["od_rope"], NT * h + t)
                    V.do(tt(r_tmp[0], x1, tabs[0], ALU.mult))
                    V.do(tt(r_tmp[1], x2, tabs[1], ALU.mult))
                    V.do(tt(r_tmp[2], x2, tabs[0], ALU.mult))
                    tt(r_tmp[3], x1, tabs[1], ALU.mult).then_inc(free, 1)
                    taken(dve, "od_qk", h, t)
                    if h:
                        filled(dve, "ret_T", h - 1, t)
                    V.do(tt(r_qk[:, t, :, 0:P], r_tmp[0], r_tmp[1], ALU.subtract))
                    tt(r_qk[:, t, :, P:2 * P], r_tmp[2], r_tmp[3], ALU.add).then_inc(S["od_rope"], 1)

            def head_norm(g):
                for t in range(NT):
                    bank, _ = filled(dve, "ret_y", g, t)
                    V.then(nc.vector.bn_stats(stats[:, t, 0], bank[:]))
                    nc.vector.bn_aggr(aggr[:, t], stats[:, t, 0]).then_inc(S["ret_var"], 1)
                for t in range(NT):
                    dve.wait_ge(S["ret_rstd"], NT * g + t + 1)
                    V.then(nc.vector.reciprocal(rstd[:, t:t + 1], rstd[:, t:t + 1]))
                    if g:
                        filled(dve, "ret_yT", g - 1, t)
                    bank, free = filled(dve, "ret_y", g, t)
                    ts(r_y[:, t], bank[:], aggr[:, t, 0:1], rstd[:, t:t + 1], ALU.subtract, ALU.mult).then_inc(free, 1)
                    taken(dve, "ret_y", g, t)
                    dve.wait_ge(S["od_gate"], NT * g + t + 1)
                    tt(r_y[:, t], r_y[:, t], r_g[:, g % 2, t], ALU.mult).then_inc(S["ret_y"], 1)

            def turned_rows(g):
                for t in range(NT):
                    to = (slice(None), slice(4 * g, 4 * g + 4), slice(t * P, (t + 1) * P))
                    rows_turned(("ret_yT", g, t), (yT_hi[to], yT_lo[to]), heads)

            dve.wait_ge(S["ret_in"], 16)
            for h in range(RH):
                split_ahead("od_qk", h)
                rotate(h)
                if h:
                    head_norm(h - 1)
                split_ahead("od_v", h)
                split_ahead("od_g", h)
                cond(1, OD_COND[h])
                bank, free = filled(dve, "ret_s", h)
                V.do(tt(r_s[:, 0:2 * P], bank[:, 0:2 * P], ret_d[:, h], ALU.mult))
                tt(r_s[:, 2 * P:3 * P], bank[:, 2 * P:3 * P], ret_d[:, h, 0:P], ALU.mult).then_inc(free, 1)
                if h:
                    turned_rows(h - 1)
            for i in range(4):
                split_ahead("od_out", i)
                if i == 0:
                    head_norm(RH - 1)
                if i == 1:
                    turned_rows(RH - 1)
            for t in range(NT):
                for half in range(2):
                    residual(1, 2, ("od_out", t, half), t, half)
            layer_norm(2)
            modulate(1, 3)
            narrow_lo(rw, 2)
            turned(4)
            for n in range(2):
                rest(0, n, 0, n)
            dve.wait_ge(S["late_in"], 16)
            bank, free = filled(dve, "router")
            tt(logit, bank[:, 0:NT * NE].rearrange("p (t e) -> p t e", t=NT), over_all(rb, NT), ALU.add).then_inc(free, 1)
            taken(dve, "router")
            iota8 = over_all(iota[:, 0:NE], NT)
            for lg, m, first, eq in ((logit, m1, i1, eq1), (l2, m2, i2, eq2)):
                V.then(nc.vector.tensor_reduce(m, lg, AX.X, ALU.max))
                V.then(tt(key_, lg, per_row(m, NE), ALU.is_equal))
                V.then(stt(key_, key_, -100.0, iota8, ALU.mult, ALU.add))
                V.then(nc.vector.tensor_reduce(first, key_, AX.X, ALU.min))
                V.then(tt(eq, key_, per_row(first, NE), ALU.is_equal))
                if lg is logit:
                    V.then(stt(l2, eq, NEG, logit, ALU.mult, ALU.add))
            tt(e12, m2, m1, ALU.subtract).then_inc(S["route_in"], 1)
            mask2 = table[:, 2:4, 0:NE]
            tt(mask2, eq1, eq2, ALU.add).then_inc(S["rank_in"], 1)
            dve.wait_ge(S["route_exp"], 1)
            V.then(ts(w1, e12, 1.0, None, ALU.add))
            V.then(nc.vector.reciprocal(w1, w1))
            V.then(tt(w2, e12, w1, ALU.mult))
            V.then(tt(eq1, eq1, per_row(w1, NE), ALU.mult))
            V.then(tt(eq2, eq2, per_row(w2, NE), ALU.mult))
            for i in range(2):
                V.do(tt(table[:, 4:6, NE * i:NE * i + NE], eq1, eq2, ALU.add))
            dve.wait_ge(S["rank_in"], 1)
            V.do(nc.vector.tensor_copy(table[:, 2:4, NE:], mask2))
            bank, free = filled(dve, "rank")
            places = bank[:, 0:NT * NE].rearrange("p (t e) -> p t e", t=NT)
            V.do(nc.vector.tensor_copy(table[:, 0:2, 0:NE], places))
            V.do(ts(table[:, 0:2, NE:], places, -float(P), None, ALU.add))
            nc.vector.tensor_copy(cnt, bank[:, NT * NE:NT * NE + NE]).then_inc(free, 1)
            taken(dve, "rank")
            V.do(nc.vector.memset(item_no, 0.0))
            V.do(nc.vector.tensor_copy(code[:, 0:NE], iota[:, 0:NE]))
            V.then(nc.vector.memset(code[:, NE:], -1.0))

            def build():
                V.then(ts(hot, code, item_no, None, ALU.is_equal))
                V.do(ts(item_no, item_no, 1.0, None, ALU.add))
                V.then(tt(pick, table, over_all(hot, 6), ALU.mult))
                V.then(nc.vector.tensor_reduce(picked, pick, AX.X, ALU.add))
                for t in range(NT):
                    V.do(ts(p_tok[:, t], iota, picked[:, t:t + 1], picked[:, 2 + t:3 + t], ALU.is_equal, ALU.mult))
                for t in range(NT):
                    last = ts(pw_tok[:, t], iota, picked[:, t:t + 1], picked[:, 4 + t:5 + t], ALU.is_equal, ALU.mult)
                    if t < NT - 1:
                        V.do(last)
                last.then_inc(S["p_ready"], 1)

            def tokens_lo(half, bank_free_, count):
                bank, free = bank_free_
                dve.wait_ge(S["tok_hi"], count)
                to = slice(4 * half, 4 * half + 4)
                tt(heT_lo[:, to], heads(bank), heT_hi[:, to].bitcast(F32), ALU.subtract).then_inc(free, 1)

            BUILD_STEPS = 7
            n0 = V.n
            build()
            assert V.n - n0 == BUILD_STEPS
            V.wait()
            V.then(ts(over, cnt, float(P), None, ALU.is_gt))
            src, dst = over, rank_o
            for d in (1, 2, 4):
                V.do(nc.vector.tensor_copy(dst[:, 0:d], src[:, 0:d]))
                V.then(tt(dst[:, d:], src[:, d:], src[:, 0:NE - d], ALU.add))
                src, dst = dst, (cnt if dst is rank_o else rank_o)
            V.then(stt(code[:, NE:], src, float(NE), over, ALU.add, ALU.mult))
            V.then(ts(code[:, NE:], code[:, NE:], -1.0, None, ALU.add))
            for i in range(MAX_OVER):
                V.then(ts(over_hot[:, i], code[:, NE:], float(NE + i), None, ALU.is_equal))
                V.do(tt(over_hot[:, i], over_hot[:, i], iota[:, 0:NE], ALU.mult))
            V.wait()
            V.do(nc.vector.tensor_copy(over_int[0:1, 3:4], src[0:1, NE - 1:NE]))
            V.then(nc.vector.tensor_reduce(over_id, over_hot, AX.X, ALU.add))
            nc.vector.tensor_copy(over_int[0:1, 0:3], over_id[0:1, :]).then_inc(S["over_ready"], 1)
            for half in range(2):
                tokens_lo(half, filled(dve, "gather", half), 1 + half)
            steps_before = V.n

            def add_back(it):
                for i in range(4):
                    item_taken(dve, it, "back", i, ago=1)
                    bank, free = item_filled(dve, it, "back", i)
                    to = ysum[:, i // 2, 512 * (i % 2):512 * (i % 2) + 512]
                    tt(to, to, bank[:], ALU.add).then_inc(free, 1)

            def item(it, late=0):
                def split_unit(u):
                    for n in (2 * (u + late), 2 * (u + late) + 1):
                        rest(it, n, n // 2 % RING, n % 3)

                if late:
                    split_unit(0)
                for u in range(N_UNITS):
                    if 1 <= u <= N_UP:
                        bank, free = item_filled(dve, it, "up", u - 1)
                        dve.wait_ge(S["e_silu"], it * N_UP + u)
                        item_filled(dve, it, "act_T", (u - 3) % N_UP, ago=int(u < 3))
                        tt(e_a[:, (u - 1) % 2], e_s[:, (u - 1) % 2], bank[:, 256:512], ALU.mult).then_inc(free, 1)
                    if u < N_UNITS - late:
                        split_unit(u + 1)
                    if u == 0:
                        add_back(it)
                        item_filled(dve, it, "pwT")
                        V.n, V.base = 0, it * BUILD_STEPS + steps_before
                        build()
                    if 1 <= u <= N_UP:
                        dve.wait_ge(S["act_hi"], it * N_UP + u)
                        bank, free = item_filled(dve, it, "act_T", u - 1)
                        to = slice(2 * u - 2, 2 * u)
                        tt(eT_lo[:, to], bank[:, 0:256].rearrange("p (j s) -> p j s", j=2),
                           eT_hi[:, to].bitcast(F32), ALU.subtract).then_inc(free, 1)
                    if u == N_UP + 1:
                        for half in range(2):
                            tokens_lo(half, item_filled(dve, it, "gather", half), it * 2 + (3 + half))

            dve.wait_ge(S["zeroed"], NT)
            with dve.Fori(0, NE) as it:
                item(it)
            over_loop(dve, lambda it: item(it, 1))
            add_back(dve.value_load(over_int[0:1, 3:4], min_val=0, max_val=MAX_OVER) + NE)
            V = Steps(dve, S["last_step"])
            V.then(nc.vector.memset(item_no, 0.0))
            for t in range(NT):
                for half in range(2):
                    residual(1, 5, None, t, half)
            layer_norm(3)

        @block.gpsimd
        def _(pool):
            tt = nc.gpsimd.tensor_tensor
            quad = lambda a, t: a[:, GH * t:GH * t + GH]
            pool.dma_start(alog, ev_a_log.broadcast_to([P, GH])).then_inc(S["gates_in"], 16)
            pool.dma_start(dtb, ev_dt_bias.broadcast_to([P, GH])).then_inc(S["gates_in"], 16)
            pool.dma_start(sinks, ev_sinks.broadcast_to([P, SH])).then_inc(S["sinks_in"], 16)
            pool.dma_start(gdnw, ev_gdn_norm_w.broadcast_to([P, GD])).then_inc(S["gdnw_in"], 16)

            def load_ln(stage):
                for i, w in enumerate((ln_w, ln_b)):
                    pool.dma_start(ln[:, i], w[stage // 2, stage % 2:stage % 2 + 1, :].broadcast_to([P, D])) \
                        .then_inc(S["ln_in"], 16)

            at = [0]

            def split_to(*key):
                end = parts_ahead(key)
                for k in split_order[at[0]:end]:
                    if low_mark[k][0] == "w_lo_pool":
                        pool.wait_ge(S["w_hi"], part_no[k] + 1)
                        tt(part_buffer(k, 1), slot_part(pool, k), part_buffer(k, 0).bitcast(F32),
                           ALU.subtract).then_inc(S["w_lo_pool"], 1)
                at[0] = end

            split_to("ev_in", 3)
            pool.wait_ge(S["qk_norm"], 2)
            for t in range(NT):
                pool.wait_ge(S["exp_row"], t + 1)
                tt(quad(qdT, t), by_tile(0, t), quad(eG, t), ALU.mult).then_inc(S["q_dec"], 1)
            pool.wait_ge(S["gdnw_in"], 16)

            def level(l):
                for t in range(NT):
                    if l == 0:
                        pool.wait_ge(S["trig_ready"], 2)
                        taken(pool, "kk", t)
                    elif l == 2:
                        pool.wait_ge(S["y0_ready"], t + 1)
                    elif l > 2:
                        filled(pool, "ax", l - 2, t)
                    tt(quad(amasks[l % 2], t), quad(aD, t), over_all(cpart["levels"][:, l * P:(l + 1) * P], GH),
                       ALU.mult).then_inc(S["level_mask"], 1)

            for l in range(4):
                level(l)
            for t in range(NT):
                taken(pool, "ev_in", 3, t)
                z = zs[:, t].rearrange("p (h d) -> p h d", h=GH)
                tt(z, z, over_all(gdnw, GH), ALU.mult).then_inc(S["z_w"], 1)
            level(4)
            level(5)
            filled(pool, "pv", NT - 1)
            load_ln(0)
            split_to("ev_out", 1)
            pool.wait_ge(S["ln_done"], NT)
            load_ln(1)
            split_to("ffn_down", 5)
            filled(pool, "ffn_down", NT - 1, 1)
            pool.dma_start(ret_d, consts[:, CONST_COLS - RH * 2 * P:].rearrange("p (h n) -> p h n", h=RH)).then_inc(S["ret_in"], 16)

            def load_gnw(h):
                pool.dma_start(gnw[:, h % 2], od_gn_w[0:1, RV * h:RV * h + RV].broadcast_to([P, RV])) \
                    .then_inc(S["gnw_in"], 16)

            for h in range(2):
                load_gnw(h)
            for h in range(RH):
                pool.wait_ge(S["gnw_in"], 16 * min(h + 2, RH))
                split_to("od_g", h)
                for t in range(NT):
                    taken(pool, "od_g", h, t)
                    tt(r_g[:, h % 2, t], r_g[:, h % 2, t], gnw[:, h % 2], ALU.mult).then_inc(S["od_gate"], 1)
                if h + 2 < RH:
                    pool.wait_ge(S["od_gate"], NT * h + NT)
                    load_gnw(h + 2)
                if h == 0:
                    pool.wait_ge(S["h_ready"], 12)
                    pool.dma_start(late, consts[:, N_FIRST:N_FIRST + 2 * P]).then_inc(S["late_in"], 16)
                    pool.dma_start(rw, moe_w_router[0].rearrange("(k p) e -> p k e", p=P)).then_inc(S["router_in"], 16)
                    pool.dma_start(rb, moe_b_router.broadcast_to([P, NE])).then_inc(S["router_in"], 16)
            split_to("od_out", 1)
            pool.wait_ge(S["ret_y"], 2 * RH)
            load_ln(2)
            split_to("od_out", 3)
            pool.wait_ge(S["ln_done"], 3 * NT)
            load_ln(3)
            filled(pool, "hT", 4, 3)
            nc.gpsimd.memset(pwT, 0.0).then_inc(S["back_zero"], 1)
            nc.gpsimd.memset(ye[:], 0.0).then_inc(S["back_zero"], 1)
            filled(pool, "router")
            for t in range(NT):
                nc.gpsimd.memset(ysum[:, t], 0.0).then_inc(S["zeroed"], 1)


_INS = ["x", "c", "positions", "cond_w", "cond_b", "ln_w", "ln_b", "ev_w_in", "ev_conv_w", "ev_a_log", "ev_dt_bias",
        "ev_gdn_norm_w", "ev_sinks", "ev_w_out", "ffn_w_up", "ffn_w_down", "od_w_in", "od_gn_w", "od_w_out",
        "moe_w_router", "moe_b_router", "moe_w_up", "moe_w_down"]


def kernel(**inputs):
    import concourse.bacc as bacc
    from concourse.bass_utils import run_bass_kernel_spmd

    nc = bacc.Bacc("TRN2", target_bir_lowering=False, num_devices=1)
    arrays = {f"in_{n}": np.ascontiguousarray(inputs[n]) for n in _INS}
    arrays["in_consts"] = np.concatenate(
        [np.asarray(v, np.float32) for v in constant_table().values()], axis=1)
    args = [nc.dram_tensor(n, a.shape, mybir.dt.from_np(a.dtype), kind="ExternalInput").ap() for n, a in arrays.items()]
    out = nc.dram_tensor("out_y", (1, SEQ, D), F32, kind="ExternalOutput").ap()
    trunk(nc, *args, out)
    r = run_bass_kernel_spmd(nc, [arrays], core_ids=[0])
    return r.results[0]["out_y"]
```
